# Optimizing a Trainium2 kernel written in Bass

```python
import jax, jax.numpy as jnp
from jax import lax
import numpy as np

D_MODEL = 1024
BATCH = 1
SEQ = 512
DEPTH = 1

CHUNK = 64
N_PREV_CHUNKS = 8
BAND = (N_PREV_CHUNKS + 1) * CHUNK
HEAD_DIM = 64
H_A = 8
H_B = 8
W_A = H_A * HEAD_DIM
W_B = H_B * HEAD_DIM
W_MIX = W_A + W_B
W_IN = 3 * W_MIX
REL_CLIP = 128
SB_BLOCK = 128
D_FF = 2816
CONV_WIDTH = 3
N_MOD = 6
EPS = 1e-6


def rms_norm(x):
    xf = x.astype(jnp.float32)
    y = xf * lax.rsqrt(jnp.mean(xf * xf, axis=-1, keepdims=True) + EPS)
    return y.astype(x.dtype)

def modulate(h, shift, scale):
    return h * (1 + scale[:, None, :]) + shift[:, None, :]

def rel_bias_band(rel_bias):
    q_pos = N_PREV_CHUNKS * CHUNK + jnp.arange(CHUNK)
    k_pos = jnp.arange(BAND)
    dist = jnp.clip(q_pos[:, None] - k_pos[None, :], -REL_CLIP, REL_CLIP) + REL_CLIP
    return rel_bias[:, dist]

def chunked_rel_attention(q, k, v, rel_bias):
    b, s, h, dh = q.shape
    n_chunks = s // CHUNK
    qc = q.reshape(b, n_chunks, CHUNK, h, dh)
    pad = ((0, 0), (N_PREV_CHUNKS, 0), (0, 0), (0, 0), (0, 0))
    kp = jnp.pad(k.reshape(b, n_chunks, CHUNK, h, dh), pad)
    vp = jnp.pad(v.reshape(b, n_chunks, CHUNK, h, dh), pad)
    band_idx = jnp.arange(n_chunks)[:, None] + jnp.arange(N_PREV_CHUNKS + 1)[None, :]
    kb = kp[:, band_idx].reshape(b, n_chunks, BAND, h, dh)
    vb = vp[:, band_idx].reshape(b, n_chunks, BAND, h, dh)
    scores = jnp.einsum("bcqhd,bckhd->bhcqk", qc, kb).astype(jnp.float32) * (dh ** -0.5)
    scores = scores + rel_bias_band(rel_bias).astype(jnp.float32)[None, :, None]
    key_chunk = (jnp.arange(n_chunks)[:, None] - N_PREV_CHUNKS
                 + (jnp.arange(BAND) // CHUNK)[None, :])
    scores = jnp.where((key_chunk >= 0)[None, None, :, None, :], scores, -jnp.inf)
    probs = jax.nn.softmax(scores, axis=-1).astype(v.dtype)
    out = jnp.einsum("bhcqk,bckhd->bcqhd", probs, vb)
    return out.reshape(b, s, h * dh)

def stick_breaking_attention(q, k, v):
    b, s, h, dh = q.shape
    scale = dh ** -0.5
    outs = []
    for blk in range(s // SB_BLOCK):
        q_start = blk * SB_BLOCK
        k_end = q_start + SB_BLOCK
        logits = jnp.einsum("bqhd,bkhd->bhqk", q[:, q_start:k_end],
                            k[:, :k_end]).astype(jnp.float32) * scale
        strict = (q_start + jnp.arange(SB_BLOCK))[:, None] > jnp.arange(k_end)[None, :]
        log_beta = jax.nn.log_sigmoid(logits)
        log_keep = jnp.where(strict, jax.nn.log_sigmoid(-logits), 0.0)
        log_tail = lax.cumsum(log_keep, axis=3, reverse=True) - log_keep
        weights = jnp.where(strict, jnp.exp(log_beta + log_tail), 0.0).astype(v.dtype)
        outs.append(jnp.einsum("bhqk,bkhd->bqhd", weights, v[:, :k_end]))
    return jnp.concatenate(outs, axis=1).reshape(b, s, h * dh)

def causal_depthwise_conv(u, w, bias):
    s = u.shape[1]
    up = jnp.pad(u, ((0, 0), (CONV_WIDTH - 1, 0), (0, 0)))
    y = w[0] * up[:, 0:s]
    for i in range(1, CONV_WIDTH):
        y = y + w[i] * up[:, i:i + s]
    return y + bias

def hybrid_layer(x, c_act, w_ada, b_ada, w_in, rel_bias, g_a, g_b, w_out,
                 w_up, conv_w, conv_b, w_down):
    b, s, _ = x.shape
    mod = c_act @ w_ada + b_ada
    shift_mix, scale_mix, gate_mix, shift_ffn, scale_ffn, gate_ffn = jnp.split(mod, N_MOD, axis=-1)

    h = modulate(rms_norm(x), shift_mix, scale_mix)
    proj = h @ w_in
    cuts = [W_A, 2 * W_A, 3 * W_A, 3 * W_A + W_B, 3 * W_A + 2 * W_B]
    qa, ka, va, qb, kb, vb = jnp.split(proj, cuts, axis=-1)
    oa = chunked_rel_attention(qa.reshape(b, s, H_A, HEAD_DIM), ka.reshape(b, s, H_A, HEAD_DIM),
                               va.reshape(b, s, H_A, HEAD_DIM), rel_bias)
    ob = stick_breaking_attention(qb.reshape(b, s, H_B, HEAD_DIM), kb.reshape(b, s, H_B, HEAD_DIM),
                                  vb.reshape(b, s, H_B, HEAD_DIM))
    mixed = jnp.concatenate([rms_norm(oa) * g_a, rms_norm(ob) * g_b], axis=-1) @ w_out
    x = x + gate_mix[:, None, :] * mixed

    h = modulate(rms_norm(x), shift_ffn, scale_ffn)
    gate, val = jnp.split(causal_depthwise_conv(h @ w_up, conv_w, conv_b), 2, axis=-1)
    x = x + gate_ffn[:, None, :] * ((jax.nn.silu(gate) * val) @ w_down)
    return x

def first_inputs(seed: int = 0) -> dict:
    key = jax.random.key(seed)
    ks = jax.random.split(key, 14)
    f32 = jnp.float32
    nrm = lambda k, shape: jax.random.normal(k, shape, dtype=f32)
    return {
        "x": nrm(ks[0], (BATCH, SEQ, D_MODEL)),
        "c": nrm(ks[1], (BATCH, D_MODEL)),
        "w_ada": nrm(ks[2], (DEPTH, D_MODEL, N_MOD * D_MODEL)) * D_MODEL ** -0.5,
        "b_ada": nrm(ks[3], (DEPTH, N_MOD * D_MODEL)) * 0.02,
        "w_in": nrm(ks[4], (DEPTH, D_MODEL, W_IN)) * D_MODEL ** -0.5,
        "rel_bias": nrm(ks[5], (DEPTH, H_A, 2 * REL_CLIP + 1)) * 0.5,
        "g_a": 1.0 + 0.1 * nrm(ks[6], (DEPTH, W_A)),
        "g_b": 1.0 + 0.1 * nrm(ks[7], (DEPTH, W_B)),
        "w_out": nrm(ks[8], (DEPTH, W_MIX, D_MODEL)) * W_MIX ** -0.5,
        "w_up": nrm(ks[9], (DEPTH, D_MODEL, 2 * D_FF)) * D_MODEL ** -0.5,
        "conv_w": nrm(ks[10], (DEPTH, CONV_WIDTH, 2 * D_FF)) * CONV_WIDTH ** -0.5,
        "conv_b": nrm(ks[11], (DEPTH, 2 * D_FF)) * 0.02,
        "w_down": nrm(ks[12], (DEPTH, D_FF, D_MODEL)) * D_FF ** -0.5,
        "final_g": 1.0 + 0.1 * nrm(ks[13], (D_MODEL,)),
    }

def first_block(x, c, w_ada, b_ada, w_in, rel_bias, g_a, g_b, w_out, w_up, conv_w,
              conv_b, w_down, final_g):
    c_act = jax.nn.silu(c)
    for l in range(DEPTH):
        x = hybrid_layer(x, c_act, w_ada[l], b_ada[l], w_in[l], rel_bias[l], g_a[l], g_b[l],
                         w_out[l], w_up[l], conv_w[l], conv_b[l], w_down[l])
    return rms_norm(x) * final_g


DEPTH_2 = 2

N_MEM = 256
MIX_WIDTH = D_MODEL
N_MEM_HEADS = 4
MEM_WIDTH = N_MEM_HEADS * HEAD_DIM
TOK_WIDTH = MIX_WIDTH - MEM_WIDTH
N_FOX_HEADS = TOK_WIDTH // HEAD_DIM
GMLP_BLOCK = 128
GMLP_GROUPS = 4
GMLP_GROUP_WIDTH = TOK_WIDTH // GMLP_GROUPS
Q_BLOCK = 128
N_A = DEPTH_2 // 2
N_B = DEPTH_2 - N_A


def rmsnorm(x, g):
    xf = x.astype(jnp.float32)
    y = xf * lax.rsqrt(jnp.mean(xf * xf, axis=-1, keepdims=True) + EPS)
    return (y * g.astype(jnp.float32)).astype(x.dtype)

def memory_attention(q_mem, mem, mem_norm, w_mem_kv):
    b, s = q_mem.shape[:2]
    kv = rmsnorm(mem, mem_norm) @ w_mem_kv
    k = kv[..., :MEM_WIDTH].reshape(b, N_MEM, N_MEM_HEADS, HEAD_DIM)
    v = kv[..., MEM_WIDTH:].reshape(b, N_MEM, N_MEM_HEADS, HEAD_DIM)
    q = q_mem.reshape(b, s, N_MEM_HEADS, HEAD_DIM)
    logits = jnp.einsum("bqhd,bkhd->bhqk", q, k).astype(jnp.float32) * (HEAD_DIM ** -0.5)
    p = jax.nn.softmax(logits, axis=-1).astype(v.dtype)
    o = jnp.einsum("bhqk,bkhd->bqhd", p, v)
    return o.reshape(b, s, MEM_WIDTH)

def gmlp_spatial_gating(u, v, v_norm, w_s, b_s):
    b, s, _ = v.shape
    n = s // GMLP_BLOCK
    vn = rmsnorm(v, v_norm).reshape(b, n, GMLP_BLOCK, GMLP_GROUPS, GMLP_GROUP_WIDTH)
    causal = jnp.tril(jnp.ones((GMLP_BLOCK, GMLP_BLOCK), dtype=bool))
    w = jnp.where(causal[None], w_s, jnp.zeros_like(w_s))
    mixed = jnp.einsum("gts,bnsgc->bntgc", w, vn) + b_s.T[None, None, :, :, None]
    return u * mixed.reshape(b, s, TOK_WIDTH)

def forgetting_attention(q, k, v, log_f_cum):
    s = q.shape[1]
    scale = HEAD_DIM ** -0.5
    c = jnp.transpose(log_f_cum, (0, 2, 1))
    outs = []
    for i in range(s // Q_BLOCK):
        q0, q1 = i * Q_BLOCK, (i + 1) * Q_BLOCK
        logits = jnp.einsum("bqhd,bkhd->bhqk", q[:, q0:q1], k[:, :q1]).astype(jnp.float32) * scale
        decay = c[:, :, q0:q1, None] - c[:, :, None, :q1]
        qpos = jnp.arange(q0, q1)[:, None]
        kpos = jnp.arange(q1)[None, :]
        logits = jnp.where(qpos >= kpos, logits + decay, -jnp.inf)
        p = jax.nn.softmax(logits, axis=-1).astype(v.dtype)
        outs.append(jnp.einsum("bhqk,bkhd->bqhd", p, v[:, :q1]))
    return jnp.concatenate(outs, axis=1)

def conv_ffn(x, w_in, conv_w, conv_b, w_out):
    s = x.shape[1]
    h = x @ w_in
    hp = jnp.pad(h, ((0, 0), (CONV_WIDTH - 1, 0), (0, 0)))
    hc = conv_b + conv_w[CONV_WIDTH - 1] * h
    for j in range(CONV_WIDTH - 1):
        hc = hc + conv_w[j] * hp[:, j:j + s]
    gate, up = hc[..., :D_FF], hc[..., D_FF:]
    return (jax.nn.silu(gate) * up) @ w_out

def second_inputs(seed: int = 0) -> dict:
    key = jax.random.key(seed)
    ks = iter(jax.random.split(key, 64))

    def nrm(shape, scale):
        return jax.random.normal(next(ks), shape, jnp.float32) * scale

    def gain(shape):
        return 1.0 + nrm(shape, 0.05)

    D = D_MODEL
    inv = D ** -0.5
    inp = {}
    inp["x"] = nrm((BATCH, SEQ, D), 1.0)
    inp["mem"] = nrm((BATCH, N_MEM, D), 1.0)
    inp["a_norm1"] = gain((N_A, D))
    inp["a_w_in"] = nrm((N_A, D, 2 * TOK_WIDTH + MEM_WIDTH), inv)
    inp["a_v_norm"] = gain((N_A, TOK_WIDTH))
    inp["a_w_s"] = nrm((N_A, GMLP_GROUPS, GMLP_BLOCK, GMLP_BLOCK), 0.5 * GMLP_BLOCK ** -0.5)
    inp["a_b_s"] = 1.0 + nrm((N_A, GMLP_GROUPS, GMLP_BLOCK), 0.1)
    inp["a_mem_norm"] = gain((N_A, D))
    inp["a_w_mem_kv"] = nrm((N_A, D, 2 * MEM_WIDTH), inv)
    inp["a_w_out"] = nrm((N_A, MIX_WIDTH, D), MIX_WIDTH ** -0.5)
    inp["a_norm2"] = gain((N_A, D))
    inp["a_ffn_in"] = nrm((N_A, D, 2 * D_FF), inv)
    inp["a_ffn_conv"] = nrm((N_A, CONV_WIDTH, 2 * D_FF), CONV_WIDTH ** -0.5)
    inp["a_ffn_conv_b"] = nrm((N_A, 2 * D_FF), 0.02)
    inp["a_ffn_out"] = nrm((N_A, D_FF, D), D_FF ** -0.5)
    inp["kv_norm"] = gain((D,))
    inp["w_kv"] = nrm((D, 2 * TOK_WIDTH + N_FOX_HEADS), inv)
    inp["b_f"] = jax.random.uniform(next(ks), (N_FOX_HEADS,), jnp.float32, 1.0, 6.0)
    inp["b_norm1"] = gain((N_B, D))
    inp["b_w_q"] = nrm((N_B, D, TOK_WIDTH + MEM_WIDTH), inv)
    inp["b_mem_norm"] = gain((N_B, D))
    inp["b_w_mem_kv"] = nrm((N_B, D, 2 * MEM_WIDTH), inv)
    inp["b_w_out"] = nrm((N_B, MIX_WIDTH, D), MIX_WIDTH ** -0.5)
    inp["b_norm2"] = gain((N_B, D))
    inp["b_ffn_in"] = nrm((N_B, D, 2 * D_FF), inv)
    inp["b_ffn_conv"] = nrm((N_B, CONV_WIDTH, 2 * D_FF), CONV_WIDTH ** -0.5)
    inp["b_ffn_conv_b"] = nrm((N_B, 2 * D_FF), 0.02)
    inp["b_ffn_out"] = nrm((N_B, D_FF, D), D_FF ** -0.5)
    inp["final_norm"] = gain((D,))
    return inp

def second_block(x, mem,
              a_norm1, a_w_in, a_v_norm, a_w_s, a_b_s, a_mem_norm, a_w_mem_kv, a_w_out,
              a_norm2, a_ffn_in, a_ffn_conv, a_ffn_conv_b, a_ffn_out,
              kv_norm, w_kv, b_f,
              b_norm1, b_w_q, b_mem_norm, b_w_mem_kv, b_w_out,
              b_norm2, b_ffn_in, b_ffn_conv, b_ffn_conv_b, b_ffn_out,
              final_norm):
    b, s, _ = x.shape
    k_sh = v_sh = log_f_cum = None
    for layer in range(DEPTH_2):
        if layer < N_A:
            i = layer
            h = rmsnorm(x, a_norm1[i])
            z = h @ a_w_in[i]
            u = jax.nn.gelu(z[..., :TOK_WIDTH])
            vv = jax.nn.gelu(z[..., TOK_WIDTH:2 * TOK_WIDTH])
            q_mem = z[..., 2 * TOK_WIDTH:]
            tok = gmlp_spatial_gating(u, vv, a_v_norm[i], a_w_s[i], a_b_s[i])
            mem_o = memory_attention(q_mem, mem, a_mem_norm[i], a_w_mem_kv[i])
            x = x + jnp.concatenate([tok, mem_o], axis=-1) @ a_w_out[i]
            x = x + conv_ffn(rmsnorm(x, a_norm2[i]), a_ffn_in[i], a_ffn_conv[i], a_ffn_conv_b[i], a_ffn_out[i])
            if layer == N_A - 1:
                kvf = rmsnorm(x, kv_norm) @ w_kv
                k_sh = kvf[..., :TOK_WIDTH].reshape(b, s, N_FOX_HEADS, HEAD_DIM)
                v_sh = kvf[..., TOK_WIDTH:2 * TOK_WIDTH].reshape(b, s, N_FOX_HEADS, HEAD_DIM)
                f_logit = kvf[..., 2 * TOK_WIDTH:].astype(jnp.float32) + b_f.astype(jnp.float32)
                log_f_cum = jnp.cumsum(jax.nn.log_sigmoid(f_logit), axis=1)
        else:
            j = layer - N_A
            h = rmsnorm(x, b_norm1[j])
            z = h @ b_w_q[j]
            q = z[..., :TOK_WIDTH].reshape(b, s, N_FOX_HEADS, HEAD_DIM)
            q_mem = z[..., TOK_WIDTH:]
            tok = forgetting_attention(q, k_sh, v_sh, log_f_cum).reshape(b, s, TOK_WIDTH)
            mem_o = memory_attention(q_mem, mem, b_mem_norm[j], b_w_mem_kv[j])
            x = x + jnp.concatenate([tok, mem_o], axis=-1) @ b_w_out[j]
            x = x + conv_ffn(rmsnorm(x, b_norm2[j]), b_ffn_in[j], b_ffn_conv[j], b_ffn_conv_b[j], b_ffn_out[j])
    return rmsnorm(x, final_norm)


def setup_inputs(seed=0):
    out = dict(first_inputs(seed))
    for name, value in second_inputs(seed + 1).items():
        if name != "x":
            out[name + "_2"] = value
    return out


def reference(
    x, c, w_ada, b_ada, w_in, rel_bias, g_a, g_b, w_out, w_up, conv_w, conv_b, w_down, final_g,
    mem_2, a_norm1_2, a_w_in_2, a_v_norm_2, a_w_s_2, a_b_s_2, a_mem_norm_2, a_w_mem_kv_2,
    a_w_out_2, a_norm2_2, a_ffn_in_2, a_ffn_conv_2, a_ffn_conv_b_2, a_ffn_out_2, kv_norm_2,
    w_kv_2, b_f_2, b_norm1_2, b_w_q_2, b_mem_norm_2, b_w_mem_kv_2, b_w_out_2, b_norm2_2,
    b_ffn_in_2, b_ffn_conv_2, b_ffn_conv_b_2, b_ffn_out_2, final_norm_2,
):
    x = first_block(
        x, c, w_ada, b_ada, w_in, rel_bias, g_a, g_b, w_out, w_up, conv_w, conv_b, w_down,
        final_g,
    )
    return second_block(
        x, mem_2, a_norm1_2, a_w_in_2, a_v_norm_2, a_w_s_2, a_b_s_2, a_mem_norm_2, a_w_mem_kv_2,
        a_w_out_2, a_norm2_2, a_ffn_in_2, a_ffn_conv_2, a_ffn_conv_b_2, a_ffn_out_2, kv_norm_2,
        w_kv_2, b_f_2, b_norm1_2, b_w_q_2, b_mem_norm_2, b_w_mem_kv_2, b_w_out_2, b_norm2_2,
        b_ffn_in_2, b_ffn_conv_2, b_ffn_conv_b_2, b_ffn_out_2, final_norm_2,
    )


_drawn_inputs = setup_inputs


def setup_inputs(seed=0):
    import zlib

    import numpy as np

    out = dict(_drawn_inputs(seed))
    spreads = {}
    factors = {'conv_b': 4.337,
     'a_v_norm_2': 6.192,
     'a_mem_norm_2': 8.0,
     'a_ffn_conv_b_2': 3.849,
     'kv_norm_2': 3.213,
     'b_norm1_2': 7.613,
     'b_mem_norm_2': 8.0,
     'b_ffn_conv_b_2': 19.194,
     'b_norm2_2': 7.546}
    for name, (base, spread) in spreads.items():
        noise = np.random.default_rng([zlib.crc32(name.encode()), seed]).standard_normal(out[name].shape)
        drawn = base * np.exp(spread * noise) if base else spread * noise
        out[name] = __import__('jax').numpy.asarray(drawn.astype(out[name].dtype))
    for name, factor in factors.items():
        out[name] = (out[name] * factor).astype(out[name].dtype)
    return out
```

```python
import concourse.bass as bass
from concourse import mybir
from contextlib import ExitStack

FP32 = mybir.dt.float32
FP32R = mybir.dt.float32r
ALU = mybir.AluOpType
ACT = mybir.ActivationFunctionType

P = 128
SEQ = 512
D = 1024
KT = D // P
NT = SEQ // P
HD = 64
DFF = 2816
FT = DFF // P
CT = 2 * FT
TOK = 768
NMEM = 256
GROUPS = 4
GW = TOK // GROUPS
FOX = TOK // HD
CHUNK_COLS = 256
NEG = -1e30
EPS = 1e-6
CLAMP = 40.0
RB = 257
RROW = 640

PHASES = [("mem_a", 2, 2), ("mem_b", 2, 2), ("w_in", 12, 12), ("w_out", 4, 4), ("up0", 22, 22),
          ("down0", 12, 4), ("a_in", 8, 8), ("a_out", 4, 4), ("up1", 22, 22), ("down1", 12, 4),
          ("kv", 8, 8), ("b_q", 4, 4), ("b_out", 4, 4), ("up2", 22, 22), ("down2", 12, 4)]
C0, G0 = {}, {}
_c = _g = 0
for _name, _nc, _ng in PHASES:
    C0[_name], G0[_name] = _c, _g
    _c, _g = _c + _nc, _g + _ng
N_CHUNKS = _c
ONE_TILE_GROUPS = [G0["a_in"] + 6, G0["a_in"] + 7, G0["kv"] + 5, G0["kv"] + 6, G0["kv"] + 7]


def first_tiles(g):
    return g + 1 - sum(x <= g for x in ONE_TILE_GROUPS)


NORMS = [("mix", 8), ("oa", 4), ("ob", 4), ("ffn0", 8), ("final_g", 8), ("a1", 8), ("a2", 8),
         ("b1", 8), ("b2", 8), ("final", 8)]
NORM = {name: i for i, (name, _) in enumerate(NORMS)}
SQ0 = {name: sum(n for _, n in NORMS[:i]) for i, (name, _) in enumerate(NORMS)}
ADD0 = {name: sum(n - 1 for _, n in NORMS[:i]) for i, (name, _) in enumerate(NORMS)}

X0 = {"w_out": 0, "down0": 4, "final_g": 8, "a_out": 16, "down1": 20, "b_out": 24, "down2": 28}
SPLITS = ["w_in", "w_out", "up0", "a_in", "a_out", "up1", "kv", "b_q", "b_out", "up2"]
SPLIT0 = {n: 8 * i for i, n in enumerate(SPLITS)}
SCALED0 = {n: 8 * i for i, n in enumerate([s for s in SPLITS if s not in ("a_out", "b_out")])}

VECTORS = [("c", 8), ("g_a", 4), ("g_b", 4), ("final_g", 8), ("a_norm1_2", 8), ("a_v_norm_2", 6),
           ("a_norm2_2", 8), ("kv_norm_2", 8), ("b_norm1_2", 8), ("b_norm2_2", 8),
           ("final_norm_2", 8), ("a_mem_norm_2", 8), ("b_mem_norm_2", 8)]
VEC0 = {name: sum(n for _, n in VECTORS[:i]) for i, (name, _) in enumerate(VECTORS)}
N_VEC = sum(n for _, n in VECTORS)
CONVS = [("conv_w", "conv_b"), ("a_ffn_conv_2", "a_ffn_conv_b_2"), ("b_ffn_conv_2", "b_ffn_conv_b_2")]
N_VEC_DMAS = len(VECTORS) + 1 + 4 * len(CONVS)

BATCHES = [("vec", 2), ("mem", 8), ("x", 8), ("vm_a", 1), ("vm_b", 1), ("v_l0", 8), ("ws", 1),
           ("v_a", 8), ("v_b", 8), ("f", 1), ("out", 8)]
TR0 = {name: sum(n for _, n in BATCHES[:i]) for i, (name, _) in enumerate(BATCHES)}

SESSIONS = [("rel", 8, True), ("mem_a", 4, False), ("fox", 12, True), ("mem_b", 4, False)]
HEAD0 = {name: sum(n for _, n, _ in SESSIONS[:i]) for i, (name, _, _) in enumerate(SESSIONS)}
HEAD_TURNS = [4 if causal else 2 for _, n, causal in SESSIONS for _ in range(n)]
TURN0 = [sum(HEAD_TURNS[:i]) for i in range(len(HEAD_TURNS))]


def program(nc, a, out):
    ctx = ExitStack()
    with ctx:
        def at(name, shape, offset, dt=FP32):
            return nc.alloc_sbuf_tensor_at(name, shape, dt, offset=offset)

        def sem(name):
            return ctx.enter_context(nc.semaphore(name))

        KB = 1024
        base = -(-nc.sbuf_base // 32) * 32
        o_x, o_act, o_w, o_m = base, base + 16 * KB, base + 48 * KB, base + 96 * KB
        o_tmp = o_m + 88 * KB
        o_small = o_tmp + 8 * KB

        x = at("x_res", [P, KT, SEQ], o_x)
        act_hi = at("act_hi", [P, KT, SEQ], o_act, FP32R)
        act_lo = at("act_lo", [P, KT, SEQ], o_act + 16 * KB, FP32R)
        probs = at("probs", [P, 2, NT, SEQ], o_act)
        probsT = at("probsT", [P, 2, NT, SEQ], o_act + 16 * KB)
        vec_rows = at("vec_rows", [P, 8, P], o_act)
        rb_rows = at("rb_rows", [8, RB], o_act + 4 * KB)
        rel_rows = at("rel_rows", [8, RROW], o_act + 4 * KB + 1056)
        sq_junk = at("sq_junk", [P, D], o_x)
        mem_scaled = at("mem_scaled", [P, 2, KT, NMEM], o_act + 8 * KB)
        vmT = at("vmT", [P, 2, 2, NMEM], o_act + 24 * KB)
        kmT_b0 = at("kmT_b0", [P, 2, NMEM], o_act + 28 * KB)
        vm_b0 = at("vm_b0", [P, 2, NMEM], o_act + 30 * KB)

        w_stage = [at(f"w_stage{s}", [P, 2048], o_w + 8 * KB * s) for s in range(2)]
        w_hi = [at(f"w_hi{s}", [P, 2048], o_w + 8 * KB * (2 + s), FP32R) for s in range(2)]
        w_lo = [at(f"w_lo{s}", [P, 2048], o_w + 8 * KB * (4 + s), FP32R) for s in range(2)]

        mid_hi = at("mid_hi", [P, FT, SEQ], o_m, FP32R)
        mid_lo = at("mid_lo", [P, FT, SEQ], o_m + 44 * KB, FP32R)
        mem_hi = at("mem_hi", [P, 2, KT, NMEM], o_m, FP32R)
        mem_lo = at("mem_lo", [P, 2, KT, NMEM], o_m + 16 * KB, FP32R)
        x_tok = at("x_tok", [P, NT, D], o_m + 32 * KB)
        qkv = at("qkv", [P, 24, SEQ], o_m)
        ada_acc = at("ada_acc", [P, 6144], o_m + 48 * KB)
        ada_stage = [at(f"ada_stage{s}", [P, 2048], o_m + (72 + 8 * s) * KB) for s in range(2)]
        v_tok = at("v_tok", [P, NT, D], o_m + 48 * KB)
        rel = at("rel", [P, 8, SEQ], o_m + 64 * KB)
        z_a = at("z_a", [P, 14, SEQ], o_m)
        vtok_a = at("vtok_a", [P, NT, TOK], o_m + 28 * KB)
        ws_raw = at("ws_raw", [P, GROUPS, P], o_m + 40 * KB)
        wsT = at("wsT", [P, GROUPS, P], o_m + 42 * KB)
        bs = at("bs", [P, GROUPS, P], o_m + 44 * KB)
        oT_a = at("oT_a", [P, KT, SEQ], o_m + 46 * KB)
        vsq_junk = at("vsq_junk", [P, TOK], o_m + 62 * KB)
        zero_bias = at("zero_bias", [P, NMEM], o_m + 86 * KB)
        kv_b = at("kv_b", [P, 12, SEQ], o_m)
        oT_b = at("oT_b", [P, KT, SEQ], o_m + 12 * KB)
        q_b = at("q_b", [P, KT, SEQ], o_m + 28 * KB)
        vtok_b = at("vtok_b", [P, NT, TOK], o_m + 44 * KB)
        decay = at("decay", [P, FOX, SEQ], o_m + 56 * KB)
        kmT_b = at("kmT_b", [P, 2, NMEM], o_m + 80 * KB)
        vm_b = at("vm_b", [P, 2, NMEM], o_m + 82 * KB)
        triext = at("triext", [P, SEQ], o_m + 84 * KB)
        y = at("y", [P, KT, SEQ], o_m)
        y_tok = at("y_tok", [P, NT, D], o_m + 16 * KB)

        tmp = at("tmp", [P, 4, SEQ], o_tmp)
        mem_tok = at("mem_tok", [P, 2, D], o_tmp)

        here = [o_small]

        def small(name, shape, dt=FP32):
            n = 4
            for s in shape[1:]:
                n *= s
            t = at(name, shape, here[0], dt)
            here[0] += -(-n // 32) * 32
            return t

        vec = small("vec", [P, 8 * P])
        ident = small("ident", [P, P])
        neg_ones = small("neg_ones", [P, P])
        neg_upper = small("neg_upper", [P, P])
        tri = small("tri", [P, P])
        strict_neg = small("strict_neg", [P, P])
        causal_neg = small("causal_neg", [P, P])
        kmT_a = small("kmT_a", [P, 2, NMEM])
        vm_a = small("vm_a", [P, 2, NMEM])
        sq_sum = small("sq_sum", [P, SEQ])
        rms = small("rms", [P, SEQ])
        mod = small("mod", [P, 48])
        stats = small("stats", [P, 48])
        neg_max, row_sum, row_inv = stats[:, 0:8], stats[:, 8:16], stats[:, 16:24]
        tok_ss, eps, one_col = stats[:, 24:28], stats[:, 28:29], stats[:, 29:30]
        tok_rms, b_f = stats[:, 30:34], stats[0:FOX, 34:35]
        sig_c = stats[:, 36:44]
        sq = tmp[:, 2:4, :]
        f_rows = tmp[0:FOX, :, :]
        lfT = tmp[:, 3, 0:NT * FOX].rearrange("p (t f) -> p t f", f=FOX)

        def gain(name, t):
            return vec[:, VEC0[name] + t:VEC0[name] + t + 1]

        def modv(section, t):
            return mod[:, 8 * section + t:8 * section + t + 1]

        SHIFT_MIX, SCALE_MIX, GATE_MIX, SHIFT_FFN, SCALE_FFN, GATE_FFN = range(6)

        bank = [ctx.enter_context(nc.psum_tensor(f"bank{i}", [P, SEQ], FP32)) for i in range(8)]

        rel_dram = nc.dram_tensor("rel_scratch", [8, P, RROW], FP32)
        decay_dram = nc.dram_tensor("decay_scratch", [FOX, SEQ], FP32)
        mem_dram = nc.dram_tensor("mem_scratch", [2, P, 2 * NMEM], FP32)

        consts_set = sem("consts_set")
        vec_loaded = sem("vec_loaded")
        x_loaded = sem("x_loaded")
        mem_loaded = sem("mem_loaded")
        rb_loaded = sem("rb_loaded")
        w_loaded = [sem(f"w_loaded{s}") for s in range(2)]
        w_hi_done = sem("w_hi_done")
        w_ready = sem("w_ready")
        tile0_done = sem("tile0_done")
        chunk_done = sem("chunk_done")
        group_free = sem("group_free")
        act_ready = sem("act_ready")
        act_hi_done = sem("act_hi_done")
        scaled = sem("scaled")
        x_ready = sem("x_ready")
        sq_ready = sem("sq_ready")
        sq_added = sem("sq_added")
        sum_ready = sem("sum_ready")
        root_ready = sem("root_ready")
        rms_ready = sem("rms_ready")
        tr_ready = sem("tr_ready")
        tr_saved = sem("tr_saved")
        ada_loaded = [sem(f"ada_loaded{s}") for s in range(2)]
        ada_added = sem("ada_added")
        c_act = sem("c_act")
        mod_summed, mod_added, mod_ready = sem("mod_summed"), sem("mod_added"), sem("mod_ready")
        mem_ss, mem_root, mem_rms = sem("mem_ss"), sem("mem_root"), sem("mem_rms")
        mem_normed, mem_hi_done, mem_split = sem("mem_normed"), sem("mem_hi_done"), sem("mem_split")
        mem_stored, mem_back = sem("mem_stored"), sem("mem_back")
        rel_flat, rel_stored, rel_back, rel_masked = (
            sem("rel_flat"), sem("rel_stored"), sem("rel_back"), sem("rel_masked"))
        q_scaled = sem("q_scaled")
        tap_started, tap_added, taps_done = sem("tap_started"), sem("tap_added"), sem("taps_done")
        gate_done, mid_done, mid_hi_done, mid_ready = (
            sem("gate_done"), sem("mid_done"), sem("mid_hi_done"), sem("mid_ready"))
        scores_ready, scores_read, probs_ready, inv_ready, probs_normed = (
            sem("scores_ready"), sem("scores_read"), sem("probs_ready"), sem("inv_ready"),
            sem("probs_normed"))
        pT_ready, pT_saved, out_ready, out_saved = (
            sem("pT_ready"), sem("pT_saved"), sem("out_ready"), sem("out_saved"))
        sb_scores, sb_clamped, sb_exped, sb_logged, sb_plus = (
            sem("sb_scores"), sem("sb_clamped"), sem("sb_exped"), sem("sb_logged"), sem("sb_plus"))
        sb_tail, sb_weights, sb_out, sb_saved = (
            sem("sb_tail"), sem("sb_weights"), sem("sb_out"), sem("sb_saved"))
        gelu_done, gm_loaded, v_ss, v_root, v_rms, v_normed = (
            sem("gelu_done"), sem("gm_loaded"), sem("v_ss"), sem("v_root"), sem("v_rms"),
            sem("v_normed"))
        gm_ready, gm_biased, gm_done, zero_set = (
            sem("gm_ready"), sem("gm_biased"), sem("gm_done"), sem("zero_set"))
        f_neg, f_clamped, f_exped, f_logged, f_plus, f_summed, f_saved = (
            sem("f_neg"), sem("f_clamped"), sem("f_exped"), sem("f_logged"), sem("f_plus"),
            sem("f_summed"), sem("f_saved"))
        tri_set, bf_loaded, decay_stored, decay_back = (
            sem("tri_set"), sem("bf_loaded"), sem("decay_stored"), sem("decay_back"))
        y_ready, out_stored = sem("y_ready"), sem("out_stored")

        def rows(name):
            w = a[name]
            w = w[0] if len(w.shape) == 3 else w
            return w.rearrange("(k p) n -> p k n", p=P)

        UP = ["w_up", "a_ffn_in_2", "b_ffn_in_2"]
        DOWN = ["w_down", "a_ffn_out_2", "b_ffn_out_2"]
        A_IN_TAIL = [(1536, 128), (1664, 128)]
        KV_TAIL = [(1024, 256), (1280, 128), (1408, 128), (1536, FOX)]

        def w_part(t, nk, ncol):
            return t[:, 0:nk * ncol].rearrange("p (k n) -> p k n", n=ncol)

        nc_block = ctx.enter_context(nc.Block())
        block = nc_block

        @block.sync
        def _(sp):
            def load(c, src, nk, ncol, slot):
                if not isinstance(c, int) or c >= 2:
                    sp.wait_ge(w_ready, c - 1)
                sp.dma_start(w_part(w_stage[slot], nk, ncol), src).then_inc(w_loaded[slot], 16)

            def cols(w, k0, k1, n0, n=CHUNK_COLS):
                return w[:, k0:k1, bass.ds(n0, n)]

            sp.dma_start(mem_tok[:, :, :], a["mem_2"][0].rearrange("(t p) d -> p t d", p=P))\
                .then_inc(mem_loaded, 16)
            sp.dma_start(x_tok[:, :, :], a["x"][0].rearrange("(t p) d -> p t d", p=P))\
                .then_inc(x_loaded, 16)
            for ph, w in (("mem_a", rows("a_w_mem_kv_2")), ("mem_b", rows("b_w_mem_kv_2"))):
                for s in range(2):
                    load(C0[ph] + s, cols(w, 0, KT, CHUNK_COLS * s), KT, CHUNK_COLS, s)

            def stream(ph, w, pairs):
                with sp.Fori(0, pairs) as i:
                    for s in range(2):
                        load(C0[ph] + 2 * i + s, cols(w, 0, KT, 2 * CHUNK_COLS * i + CHUNK_COLS * s),
                             KT, CHUNK_COLS, s)

            def stream_up(f):
                w = rows(UP[f])
                with sp.Fori(0, FT // 2) as i:
                    for s in range(2):
                        load(C0[f"up{f}"] + 2 * i + s, cols(w, 0, KT, CHUNK_COLS * i + DFF * s),
                             KT, CHUNK_COLS, s)

            def stream_down(f):
                w = rows(DOWN[f])
                with sp.Fori(0, 2) as i:
                    for j in range(6):
                        k0 = 8 * (j % 3)
                        k1 = min(k0 + 8, FT)
                        load(C0[f"down{f}"] + 6 * i + j,
                             cols(w, k0, k1, 2 * CHUNK_COLS * i + CHUNK_COLS * (j // 3)),
                             k1 - k0, CHUNK_COLS, j % 2)

            def tail(ph, w, done, parts):
                for j, (n0, n) in enumerate(parts):
                    load(C0[ph] + done + j, w[:, :, n0:n0 + n], KT, n, j % 2)

            stream("w_in", rows("w_in"), 6)
            stream("w_out", rows("w_out"), 2)
            stream_up(0)
            stream_down(0)
            stream("a_in", rows("a_w_in_2"), 3)
            tail("a_in", rows("a_w_in_2"), 6, A_IN_TAIL)
            stream("a_out", rows("a_w_out_2"), 2)
            stream_up(1)
            stream_down(1)
            stream("kv", rows("w_kv_2"), 2)
            tail("kv", rows("w_kv_2"), 4, KV_TAIL)
            stream("b_q", rows("b_w_q_2"), 2)
            stream("b_out", rows("b_w_out_2"), 2)
            stream_up(2)
            stream_down(2)
            for t in range(NT):
                sp.wait_ge(tr_saved, TR0["out"] + 2 * t + 2)
                sp.dma_start(out[0, P * t:P * (t + 1), :], y_tok[:, t, :]).then_inc(out_stored, 16)
            sp.wait_ge(out_stored, 16 * NT)

        @block.gpsimd
        def _(pool):
            ones = [(ident, 0.0), (neg_upper, -1.0), (tri, 1.0), (strict_neg, 0.0), (causal_neg, 0.0)]
            for t, v in ones:
                pool.memset(t[:, :], v).then_inc(consts_set, 1)
            pool.memset(neg_ones[:, :], -1.0).then_inc(consts_set, 1)
            pool.memset(eps, EPS).then_inc(consts_set, 1)
            pool.memset(one_col, 1.0).then_inc(consts_set, 1)
            pool.memset(ada_acc[:, :], 0.0).then_inc(consts_set, 1)
            pool.wait_ge(consts_set, 9)
            for t, op, fill, first, step, mult in (
                    (ident, ALU.not_equal, 1.0, 0, -1, 1),
                    (neg_upper, ALU.is_ge, 0.0, 0, -1, 1),
                    (tri, ALU.is_ge, 0.0, 0, 1, -1),
                    (strict_neg, ALU.is_ge, NEG, -1, 1, -1),
                    (causal_neg, ALU.is_ge, NEG, 0, -1, 1)):
                pool.affine_select(out=t[:, :], in_=t[:, :], compare_op=op, fill=fill, base=first,
                                   pattern=[[step, P]], channel_multiplier=mult).then_inc(consts_set, 1)

            def ada(n, src):
                if n >= 2:
                    pool.wait_ge(ada_added, n - 1)
                pool.dma_start(ada_stage[n % 2][:, :], src).then_inc(ada_loaded[n % 2], 16)

            w_ada = a["w_ada"][0]
            for k in range(KT):
                ada(k, w_ada[P * k:P * (k + 1), 0:2048])

            pool.wait_ge(group_free, G0["mem_b"] + 1)
            pool.wait_ge(tr_saved, TR0["vm_b"] + 1)
            pool.dma_start(mem_dram.ap()[0], kmT_b0[:, :, :].rearrange("p a b -> p (a b)")).then_inc(mem_stored, 16)
            pool.dma_start(mem_dram.ap()[1], vm_b0[:, :, :].rearrange("p a b -> p (a b)")).then_inc(mem_stored, 16)

            pool.wait_ge(rel_flat, 3)
            pool.dma_start(rel_dram.ap(), rel_rows[:, :].rearrange("h (o z) -> h o z", o=1)
                           .to_broadcast([8, P, RROW])).then_inc(rel_stored, 16)
            for k in range(KT):
                for s in range(2):
                    ada(8 + 2 * k + s, w_ada[P * k:P * (k + 1), 2048 * (s + 1):2048 * (s + 2)])
            pool.wait_ge(rel_stored, 16)
            pool.wait_ge(mod_summed, 2)
            pool.dma_start(rel[:, :, :], bass.AP(tensor=rel_dram.ap().tensor, offset=P - 1,
                                                 ap=[[RROW - 1, P], [P * RROW, 8], [1, SEQ]]))\
                .then_inc(rel_back, 16)

            pool.wait_ge(chunk_done, C0["a_in"])
            pool.dma_start(ws_raw[:, :, :], a["a_w_s_2"][0].rearrange("g t s -> t g s")).then_inc(gm_loaded, 16)
            pool.dma_start(bs[:, :, :].rearrange("p g t -> p (g t)"),
                           a["a_b_s_2"][0].rearrange("g t -> (g t)").rearrange("(o n) -> o n", o=1)
                           .to_broadcast([P, GROUPS * P])).then_inc(gm_loaded, 16)

            pool.wait_ge(chunk_done, C0["kv"])
            pool.wait_ge(mem_stored, 32)
            pool.dma_start(kmT_b[:, :, :].rearrange("p a b -> p (a b)"), mem_dram.ap()[0]).then_inc(mem_back, 16)
            pool.dma_start(vm_b[:, :, :].rearrange("p a b -> p (a b)"), mem_dram.ap()[1]).then_inc(mem_back, 16)
            pool.wait_ge(f_saved, 1)
            pool.dma_start(decay_dram.ap(), decay[0:FOX, 0, :]).then_inc(decay_stored, 16)
            pool.wait_ge(decay_stored, 16)
            pool.dma_start(decay[:, :, :], bass.AP(tensor=decay_dram.ap().tensor, offset=0,
                                                   ap=[[0, P], [SEQ, FOX], [1, SEQ]])).then_inc(decay_back, 16)

        def head_rows(t, n):
            return t[HD * (n % 2):HD * (n % 2) + HD, n // 2, :]

        def session(name):
            heads = []
            for n in range({s: m for s, m, _ in SESSIONS}[name]):
                if name == "rel":
                    h = dict(q=head_rows(qkv[:, 0:4, :], n), k=head_rows(qkv[:, 4:8, :], n),
                             v=lambda kj, n=n: v_tok[:, kj, HD * n:HD * (n + 1)],
                             bias=lambda qi, n=n: rel[:, n, SEQ - P * (qi + 1):SEQ],
                             out=head_rows(qkv[:, 8:12, :], n))
                elif name == "fox":
                    h = dict(q=head_rows(q_b, n), k=head_rows(kv_b[:, 0:6, :], n),
                             v=lambda kj, n=n: vtok_b[:, kj, HD * n:HD * (n + 1)],
                             bias=lambda qi, n=n: decay[:, n, 0:P * (qi + 1)],
                             out=head_rows(oT_b, n))
                else:
                    km, vm, q, o = ((kmT_a, vm_a, z_a[:, 12:14, :], oT_a) if name == "mem_a" else
                                    (kmT_b, vm_b, q_b[:, 6:8, :], oT_b))
                    h = dict(q=head_rows(q, n), k=head_rows(km, n),
                             v=lambda kj, n=n, vm=vm: vm[:, kj, HD * n:HD * (n + 1)],
                             bias=lambda qi: zero_bias[:, :], out=head_rows(o[:, 6:8, :], n))
                causal = name in ("rel", "fox")
                h.update(head=HEAD0[name] + n, turn=TURN0[HEAD0[name] + n],
                         causal=causal, mask=name == "fox", part=HD * (n % 2),
                         keys=[P * (qi + 1) if causal else NMEM for qi in range(NT)],
                         turns=4 if causal else 2)
                heads.append(h)
            return heads

        def pairs(heads):
            return list(zip(heads + [None], [None] + heads))

        def query0(h, kj):
            return P * kj if h["causal"] else 0

        SB_STEPS = 4 * 8

        def sb_step(j):
            n, r = j // 4, j % 4
            return n, r, 3 - r, P * (3 - r)

        def gm_parts(ct):
            cuts = sorted({0, P} | {GW * g - P * ct for g in range(GROUPS) if 0 < GW * g - P * ct < P})
            return [(lo, hi, (P * ct + lo) // GW) for lo, hi in zip(cuts, cuts[1:])]

        def gm_count(ct):
            return sum(len(gm_parts(t)) for t in range(ct + 1))

        def sb_save(act, n):
            act.wait_ge(sb_out, n + 1)
            part = HD * (n % 2)
            act.activation(head_rows(qkv[:, 20:24, :], n), bank[n % 2][part:part + HD, :], ACT.Copy)\
                .then_inc(sb_saved, 1)

        def direct(act, ph, src):
            if ph == "a_out":
                act.wait_ge(gm_done, 6)
                act.wait_ge(out_saved, HEAD0["fox"])
            else:
                act.wait_ge(out_saved, HEAD0["mem_b"] + 4)
            for t in range(KT):
                act.activation(act_hi[:, t, :], src[:, t, :], ACT.Copy).then_inc(act_hi_done, 1)

        @block.tensor
        def _(pe):
            def chunk(c, slot, nk, ncol, moving, g=None, gslot=0, start=True, stop=True, n=SEQ,
                      k0=0, tile_wait=None, chunk_wait=None):
                pe.wait_ge(w_ready, c + 1)
                if start and (not isinstance(g, int) or g >= 2):
                    pe.wait_ge(group_free, g - 1)
                if chunk_wait:
                    pe.wait_ge(*chunk_wait)
                hi, lo = w_part(w_hi[slot], nk, ncol), w_part(w_lo[slot], nk, ncol)
                tiles = -(-ncol // P)
                for m in range(tiles):
                    w = min(P, ncol - P * m)
                    dst = bank[2 * gslot + m][0:w, 0:n]
                    for k in range(nk):
                        if tile_wait is not None and m == 0:
                            pe.wait_ge(act_ready, tile_wait + k + 1)
                        mh, ml = moving(k0 + k)
                        wh, wl = hi[:, k, P * m:P * m + w], lo[:, k, P * m:P * m + w]
                        pe.matmul(dst, wh, mh, start=start and k == 0, stop=False)
                        pe.matmul(dst, wh, ml, start=False, stop=False)
                        last = pe.matmul(dst, wl, mh, start=False, stop=stop and k == nk - 1)
                    if m == 0 and tiles == 2 and stop:
                        last.then_inc(tile0_done, 1)
                last.then_inc(chunk_done, 1)

            def act(k):
                return act_hi[:, k, :], act_lo[:, k, :]

            def mid(k):
                return mid_hi[:, k, :], mid_lo[:, k, :]

            def gemm_pairs(ph, n):
                with pe.Fori(0, n) as i:
                    for s in range(2):
                        chunk(C0[ph] + 2 * i + s, s, KT, CHUNK_COLS, act, g=G0[ph] + 2 * i + s,
                              gslot=s, tile_wait=SPLIT0[ph])

            def gemm_down(f):
                with pe.Fori(0, 2) as i:
                    for j in range(6):
                        k0 = 8 * (j % 3)
                        k1 = min(k0 + 8, FT)
                        chunk(C0[f"down{f}"] + 6 * i + j, j % 2, k1 - k0, CHUNK_COLS, mid,
                              g=G0[f"down{f}"] + 2 * i + j // 3, gslot=j // 3, start=j % 3 == 0,
                              stop=j % 3 == 2, k0=k0, chunk_wait=(mid_ready, FT * f + k1))

            def batch(name, b, parts, wait=None):
                n = TR0[name] + b
                if n >= 2:
                    pe.wait_ge(tr_saved, n - 1)
                if wait:
                    pe.wait_ge(*wait)
                for src, c0 in parts:
                    r, w = src.shape[0], src.shape[1]
                    last = pe.transpose(bank[6 + n % 2][0:w, c0:c0 + r], src, ident[0:r, 0:r])
                last.then_inc(tr_ready, 1)

            def norm_sum(name):
                n = NORM[name]
                pe.wait_ge(sq_added, ADD0[name] + NORMS[n][1] - 1)
                if n:
                    pe.wait_ge(root_ready, n)
                pe.matmul(bank[5][:, :], neg_ones[:, :], sq_sum[:, :], start=True, stop=True)\
                    .then_inc(sum_ready, 1)

            def softmax(name):
                for nxt, cur in pairs(session(name)):
                    for i in range(4):
                        if nxt:
                            j = 4 * nxt["head"] + i
                            if j >= 4:
                                pe.wait_ge(scores_read, j - 3)
                            dst = bank[2 + j % 4][:, 0:nxt["keys"][i]]
                            q = nxt["q"][:, P * i:P * (i + 1)]
                            last = pe.matmul(dst, q, nxt["k"][:, 0:nxt["keys"][i]], start=True,
                                             stop=True)
                            if nxt["mask"]:
                                last = pe.matmul(bank[2 + j % 4][:, P * i:P * (i + 1)], ident[:, :],
                                                 causal_neg[:, :], start=False, stop=True,
                                                 skip_group_check=True)
                            last.then_inc(scores_ready, 1)
                        if cur and i < cur["turns"]:
                            t = cur["turn"] + i
                            if t >= 2:
                                pe.wait_ge(pT_saved, t - 1)
                            first = i if cur["causal"] else 0
                            for qi in range(first, NT):
                                pe.wait_ge(probs_normed, 4 * cur["head"] + qi + 1)
                                last = pe.transpose(bank[6 + t % 2][:, P * qi:P * (qi + 1)],
                                                    probs[:, cur["head"] % 2, qi, P * i:P * (i + 1)],
                                                    ident[:, :])
                            last.then_inc(pT_ready, 1)
                        if cur and 1 <= i:
                            values(cur, i - 1)
                    if cur and cur["turns"] == 4:
                        values(cur, 3)

            def values(h, kj):
                if kj >= h["turns"]:
                    return
                pe.wait_ge(pT_saved, h["turn"] + kj + 1)
                if kj == 0 and h["head"] >= 2:
                    pe.wait_ge(out_saved, h["head"] - 1)
                q0 = query0(h, kj)
                last = pe.matmul(bank[h["head"] % 2][h["part"]:h["part"] + HD, q0:SEQ], h["v"](kj),
                                 probsT[:, h["head"] % 2, kj, q0:SEQ], start=kj == 0,
                                 stop=True, skip_group_check=True)
                if kj == h["turns"] - 1:
                    last.then_inc(out_ready, 1)

            def sb_qk(j):
                n, r, kj, q0 = sb_step(j)
                if j >= 6:
                    pe.wait_ge(sb_weights, j - 5)
                b = bank[2 + j % 6]
                k = head_rows(qkv[:, 16:20, :], n)[:, P * kj:P * (kj + 1)]
                pe.matmul(b[:, q0:SEQ], k, head_rows(qkv[:, 12:16, :], n)[:, q0:SEQ], start=True,
                          stop=True, skip_group_check=True)
                pe.matmul(b[:, q0:q0 + P], ident[:, :], strict_neg[:, :], start=False, stop=True,
                          skip_group_check=True).then_inc(sb_scores, 1)

            def sb_tail_sum(j):
                n, r, kj, q0 = sb_step(j)
                pe.wait_ge(sb_plus, j + 1)
                b = bank[2 + j % 6]
                last = pe.matmul(b[:, q0:SEQ], neg_upper[:, :], probs[:, n % 2, r, q0:SEQ],
                                 start=False, stop=True, skip_group_check=True)
                for older in range(r):
                    p0 = P * (3 - older)
                    last = pe.matmul(b[:, p0:SEQ], neg_ones[:, :], probs[:, n % 2, older, p0:SEQ],
                                     start=False, stop=True, skip_group_check=True)
                last.then_inc(sb_tail, 1)

            def sb_values(n):
                if n >= 2:
                    pe.wait_ge(sb_saved, n - 1)
                pe.wait_ge(sb_weights, 4 * n + 4)
                part = HD * (n % 2)
                for kj in range(4):
                    last = pe.matmul(bank[n % 2][part:part + HD, P * kj:SEQ],
                                     v_tok[:, kj, 512 + HD * n:512 + HD * (n + 1)],
                                     probsT[:, n % 2, kj, P * kj:SEQ], start=kj == 0, stop=True,
                                     skip_group_check=True)
                last.then_inc(sb_out, 1)

            def ada_sum(cols, which):
                for j in cols:
                    last = pe.matmul(bank[5][:, j:j + 1], ada_acc[:, P * j:P * (j + 1)], one_col,
                                     start=True, stop=True)
                last.then_inc(mod_summed, 1)

            pe.wait_ge(consts_set, 14)
            pe.wait_ge(vec_loaded, 16 * N_VEC_DMAS)
            sizes = [N_VEC, 48] + [2 * CT] * 6
            for b in range(2):
                batch("vec", b, [(vec_rows[0:sizes[i], i, :], P * (i % 4)) for i in range(4 * b, 4 * b + 4)])
            pe.wait_ge(mem_normed, 2)
            for k in range(KT):
                batch("mem", k, [(mem_tok[:, t, P * k:P * (k + 1)], P * t) for t in range(2)])
            pe.wait_ge(x_loaded, 16)
            for k in range(KT):
                batch("x", k, [(x_tok[:, t, P * k:P * (k + 1)], P * t) for t in range(NT)])
            for l, ph in enumerate(("mem_a", "mem_b")):
                for s in range(2):
                    chunk(C0[ph] + s, s, KT, CHUNK_COLS,
                          lambda k, l=l: (mem_hi[:, l, k, :], mem_lo[:, l, k, :]), g=G0[ph] + s,
                          gslot=s, n=NMEM, chunk_wait=(mem_split, l + 1))
            for l, name in enumerate(("vm_a", "vm_b")):
                batch(name, 0, [(vmT[:, l, m, P * t:P * (t + 1)], NMEM * t + P * m)
                                for t in range(2) for m in range(2)], wait=(group_free, 2 * l + 2))
            norm_sum("mix")
            pe.wait_ge(root_ready, 1)
            pe.wait_ge(ada_added, 8)
            ada_sum(range(16), 0)
            gemm_pairs("w_in", 6)
            pe.wait_ge(ada_added, 24)
            pe.wait_ge(mod_ready, 1)
            ada_sum(range(16, 48), 1)
            pe.wait_ge(group_free, G0["w_out"])
            for b in range(8):
                half, t = b // 4, b % 4
                batch("v_l0", b, [(qkv[:, 8 + 12 * half + m, P * t:P * (t + 1)], P * m) for m in range(4)],
                      wait=(mod_ready, 2) if b == 0 else None)
            pe.wait_ge(tr_saved, TR0["v_l0"] + 8)
            pe.wait_ge(q_scaled, 2)
            softmax("rel")
            pe.wait_ge(out_saved, 8)
            sb_qk(0)
            sb_qk(1)
            for j in range(SB_STEPS):
                if j + 2 < SB_STEPS:
                    sb_qk(j + 2)
                sb_tail_sum(j)
                if j % 4 == 1 and j > 4:
                    sb_values(j // 4 - 1)
            sb_values(7)
            norm_sum("oa")
            norm_sum("ob")
            gemm_pairs("w_out", 2)
            norm_sum("ffn0")
            gemm_pairs("up0", FT // 2)
            gemm_down(0)
            norm_sum("final_g")
            norm_sum("a1")
            gemm_pairs("a_in", 3)
            for j, (_, n) in enumerate(A_IN_TAIL):
                chunk(C0["a_in"] + 6 + j, j, KT, n, act, g=G0["a_in"] + 6 + j, gslot=j)
            batch("ws", 0, [(ws_raw[:, g, :], P * g) for g in range(GROUPS)], wait=(gm_loaded, 32))
            for b in range(8):
                t, half = b // 2, b % 2
                batch("v_a", b, [(z_a[:, 6 + 3 * half + m, P * t:P * (t + 1)], P * m) for m in range(3)],
                      wait=(gelu_done, 6))
            pe.wait_ge(v_normed, 4)
            pe.wait_ge(group_free, G0["a_out"])
            for ct in range(6):
                if ct >= 4:
                    pe.wait_ge(gm_biased, gm_count(ct - 4))
                for lo, hi, g in gm_parts(ct):
                    for t in range(NT):
                        last = pe.matmul(bank[ct % 4][lo:hi, P * t:P * (t + 1)],
                                         vtok_a[:, t, P * ct + lo:P * ct + hi], wsT[:, g, :],
                                         start=True, stop=True, skip_group_check=True)
                last.then_inc(gm_ready, 1)
            pe.wait_ge(gm_biased, gm_count(5))
            pe.wait_ge(zero_set, 1)
            softmax("mem_a")
            pe.wait_ge(out_saved, HEAD0["fox"])
            gemm_pairs("a_out", 2)
            norm_sum("a2")
            gemm_pairs("up1", FT // 2)
            gemm_down(1)
            norm_sum("b1")
            gemm_pairs("kv", 2)
            for j, (_, n) in enumerate(KV_TAIL):
                chunk(C0["kv"] + 4 + j, j % 2, KT, n, act, g=G0["kv"] + 4 + j, gslot=j % 2)
            pe.wait_ge(group_free, G0["b_q"])
            for b in range(8):
                t, half = b // 2, b % 2
                batch("v_b", b, [(kv_b[:, 6 + 3 * half + m, P * t:P * (t + 1)], P * m) for m in range(3)])
            batch("f", 0, [(f_rows[:, 1, P * t:P * (t + 1)], FOX * t) for t in range(NT)], wait=(f_plus, 1))
            pe.wait_ge(tr_saved, TR0["f"] + 1)
            pe.wait_ge(tri_set, 2)
            for t in range(NT):
                last = pe.matmul(bank[4][0:FOX, P * t:SEQ], lfT[:, t, :], triext[:, 0:SEQ - P * t],
                                 start=t == 0, stop=True, skip_group_check=True)
            last.then_inc(f_summed, 1)
            gemm_pairs("b_q", 2)
            pe.wait_ge(group_free, G0["b_out"])
            pe.wait_ge(q_scaled, 4)
            pe.wait_ge(f_saved, 1)
            softmax("fox")
            pe.wait_ge(mem_back, 32)
            softmax("mem_b")
            pe.wait_ge(out_saved, HEAD0["mem_b"] + 4)
            gemm_pairs("b_out", 2)
            norm_sum("b2")
            gemm_pairs("up2", FT // 2)
            gemm_down(2)
            norm_sum("final")
            for b in range(8):
                t, half = b // 2, b % 2
                batch("out", b, [(y[:, 4 * half + m, P * t:P * (t + 1)], P * m) for m in range(4)],
                      wait=(y_ready, 4 * half + 4))

        @block.scalar
        def _(act):
            def split_w(c, slot, count, n=2048):
                act.wait_ge(w_loaded[slot], count)
                if not isinstance(c, int) or c >= 2:
                    act.wait_ge(chunk_done, c - 1)
                act.activation(w_hi[slot][:, 0:n], w_stage[slot][:, 0:n], ACT.Copy).then_inc(w_hi_done, 1)

            def split_at(c, n=2048):
                split_w(c, c % 2, 16 * (c // 2 + 1), n)

            def split_loop(c0, i, s):
                split_w(c0 + 2 * i + s, s, 16 * i + 16 * (c0 // 2 + 1))

            def squares(name, tile, ready):
                n, count = NORM[name], NORMS[NORM[name]][1]
                for t in range(count):
                    square(name, t, tile(t), ready(t))

            def square(name, t, src, ready):
                n = NORM[name]
                act.wait_ge(*ready)
                if t == 0:
                    if n:
                        act.wait_ge(sum_ready, n)
                    act.activation(sq_sum[:, :], src, ACT.Square).then_inc(sq_ready, 1)
                else:
                    if t >= 3:
                        act.wait_ge(sq_added, ADD0[name] + t - 2)
                    act.activation(sq[:, t % 2, :], src, ACT.Square).then_inc(sq_ready, 1)

            def root(name):
                n, count = NORM[name], NORMS[NORM[name]][1]
                act.wait_ge(sum_ready, n + 1)
                act.activation(rms[:, :], bank[5][:, :], ACT.Sqrt, scale=-1.0 / (P * count), bias=eps)\
                    .then_inc(root_ready, 1)

            def high(name, t, bias=None):
                act.wait_ge(scaled, SCALED0[name] + t + 1)
                act.activation(act_hi[:, t, :], tmp[:, t % 4, :], ACT.Identity,
                               bias=bias if bias is not None else 0.0).then_inc(act_hi_done, 1)

            def exps(h, i):
                j = 4 * h["head"] + i
                act.wait_ge(scores_read, j + 1)
                if h["head"] >= 2 and i == 0:
                    act.wait_ge(pT_ready, TURN0[h["head"] - 1])
                n = h["keys"][i]
                act.activation(probs[:, h["head"] % 2, i, 0:n], tmp[:, j % 4, 0:n], ACT.Exp, scale=-1.0,
                               bias=neg_max[:, j % 8:j % 8 + 1],
                               accum_out=row_sum[:, j % 8:j % 8 + 1]).then_inc(probs_ready, 1)

            def save_pT(h, kj):
                t = h["turn"] + kj
                act.wait_ge(pT_ready, t + 1)
                if h["head"] >= 2 and kj == 0:
                    act.wait_ge(out_ready, h["head"] - 1)
                q0 = query0(h, kj)
                act.activation(probsT[:, h["head"] % 2, kj, q0:SEQ], bank[6 + t % 2][:, q0:SEQ],
                               ACT.Copy).then_inc(pT_saved, 1)

            def softmax(name):
                for nxt, cur in pairs(session(name)):
                    for i in range(4):
                        if nxt:
                            exps(nxt, i)
                        if cur and i < cur["turns"]:
                            save_pT(cur, i)
                    if cur:
                        act.wait_ge(out_ready, cur["head"] + 1)
                        act.activation(cur["out"], bank[cur["head"] % 2][cur["part"]:cur["part"] + HD, :],
                                       ACT.Copy).then_inc(out_saved, 1)

            def softplus(t, clamped, exped, logged, n):
                act.wait_ge(clamped, n)
                act.activation(t, t, ACT.Exp).then_inc(exped, 1)
                act.wait_ge(exped, n)
                act.activation(t, t, ACT.Ln, bias=1.0).then_inc(logged, 1)

            def up(f):
                c0, g0, n0 = C0[f"up{f}"], G0[f"up{f}"], FT // 2 * f
                vb = P * (3 + 2 * f)
                act.preload_act_table(ACT.Silu)
                with act.Fori(0, FT // 2) as i:
                    for s in range(2):
                        split_loop(c0 + 2, i, s)
                        for m in range(2):
                            if m == 0:
                                act.wait_ge(tile0_done, 2 * i + s + first_tiles(g0))
                                if s == 0:
                                    act.wait_ge(mid_ready, 2 * i + 2 * n0)
                            else:
                                act.wait_ge(chunk_done, 2 * i + s + c0 + 1)
                            w2 = vec[:, bass.ds(2 * i + vb + FT * s + m, 1)]
                            b = vec[:, bass.ds(2 * i + vb + CT + FT * s + m, 1)]
                            act.activation(tmp[:, 2 * s + m, :], bank[2 * s + m][:, :], ACT.Identity,
                                           scale=w2, bias=b).then_inc(tap_started, 1)
                    for m in range(2):
                        if m == 0:
                            act.wait_ge(taps_done, 2 * i + 2 * n0 + 1)
                        else:
                            act.wait_ge(group_free, 2 * i + g0 + 1)
                        act.activation(tmp[:, m, :], tmp[:, m, :], ACT.Silu).then_inc(gate_done, 1)
                    for m in range(2):
                        act.wait_ge(mid_done, 2 * n0 + 2 * i + m + 1)
                        act.activation(mid_hi[:, bass.ds(2 * i + m, 1), :], tmp[:, m, :], ACT.Copy)\
                            .then_inc(mid_hi_done, 1)

            def updated(ph, t):
                if t % 2:
                    return group_free, G0[ph] + t // 2 + 1
                return x_ready, X0[ph] + t // 2 + 1

            def down(f, name):
                def split_next(n):
                    if C0[f"down{f}"] + n < N_CHUNKS:
                        split_at(C0[f"down{f}"] + n,
                                 6 * CHUNK_COLS if n % 3 == 2 and n < 12 else 2048)
                for g in range(4):
                    for r in range(2):
                        split_next(3 * g + r + 2)
                    for m in range(2):
                        t = 2 * g + m
                        square(name, t, x[:, t, :], updated(f"down{f}", t))
                    split_next(3 * g + 4)

            def out_phase(ph, name):
                for g in range(4):
                    for m in range(2):
                        t = 2 * g + m
                        square(name, t, x[:, t, :], updated(ph, t))
                    split_at(C0[ph] + g + 2)

            for name, n in VECTORS:
                src = a[name].rearrange("o (k p) -> (o k) p", p=P) if len(a[name].shape) == 2 else \
                    a[name].rearrange("(k p) -> k p", p=P)
                act.dma_start(vec_rows[VEC0[name]:VEC0[name] + n, 0, :], src).then_inc(vec_loaded, 16)
            act.dma_start(vec_rows[0:48, 1, :], a["b_ada"].rearrange("o (k p) -> (o k) p", p=P))\
                .then_inc(vec_loaded, 16)
            for f, (w, b) in enumerate(CONVS):
                for j in range(3):
                    act.dma_start(vec_rows[CT * (j % 2):CT * (j % 2) + CT, 2 + 2 * f + j // 2, :],
                                  a[w][0, j, :].rearrange("(k p) -> k p", p=P)).then_inc(vec_loaded, 16)
                act.dma_start(vec_rows[CT:2 * CT, 3 + 2 * f, :],
                              a[b].rearrange("o (k p) -> (o k) p", p=P)).then_inc(vec_loaded, 16)
            act.dma_start(rb_rows[:, :], a["rel_bias"][0]).then_inc(rb_loaded, 16)
            act.dma_start(b_f, a["b_f_2"].rearrange("(f o) -> f o", o=1)).then_inc(bf_loaded, 16)
            act.wait_ge(mem_loaded, 16)
            act.wait_ge(consts_set, 14)
            for t in range(2):
                if t:
                    act.wait_ge(mem_ss, t)
                act.activation(sq_junk[:, :], mem_tok[:, t, :], ACT.Square,
                               accum_out=tok_ss[:, t:t + 1]).then_inc(mem_ss, 1)
            act.wait_ge(mem_ss, 2)
            act.activation(tok_rms[:, 0:2], tok_ss[:, 0:2], ACT.Sqrt, scale=1.0 / D, bias=eps)\
                .then_inc(mem_root, 1)
            split_at(0)
            split_at(1)
            act.wait_ge(tr_saved, TR0["vec"] + 1)
            act.activation(sig_c, vec[:, VEC0["c"]:VEC0["c"] + 8], ACT.Silu).then_inc(c_act, 1)
            act.wait_ge(tr_saved, TR0["mem"] + 8)
            for l in range(2):
                act.activation(mem_hi[:, l, :, :], mem_scaled[:, l, :, :], ACT.Copy).then_inc(mem_hi_done, 1)
            squares("mix", lambda t: x[:, t, :], lambda t: (tr_saved, TR0["x"] + t + 1))
            for c in range(4):
                split_at(c + 2)
            root("mix")
            act.wait_ge(mem_stored, 32)
            act.wait_ge(rel_stored, 16)
            for t in range(KT):
                high("w_in", t, bias=modv(SHIFT_MIX, t))
            with act.Fori(0, 6) as i:
                for s in range(2):
                    split_loop(C0["w_in"] + 2, i, s)
            for n, t in enumerate((0, 12)):
                act.wait_ge(group_free, G0["w_in"] + t // 2 + 2)
                act.activation(qkv[:, t:t + 4, :], qkv[:, t:t + 4, :], ACT.Copy, scale=HD ** -0.5)\
                    .then_inc(q_scaled, 1)
            act.wait_ge(chunk_done, C0["w_out"])
            softmax("rel")
            act.preload_act_table_set("natural_log_exp_and_others")
            for j in range(SB_STEPS + 2):
                if j < SB_STEPS:
                    n, r, kj, q0 = sb_step(j)
                    softplus(tmp[:, j % 4, q0:SEQ], sb_clamped, sb_exped, sb_logged, j + 1)
                if j >= 2:
                    i = j - 2
                    n, r, kj, q0 = sb_step(i)
                    act.wait_ge(sb_tail, i + 1)
                    if n >= 2 and r == 0:
                        act.wait_ge(sb_out, n - 1)
                    act.activation(probsT[:, n % 2, kj, q0:SEQ], bank[2 + i % 6][:, q0:SEQ], ACT.Exp)\
                        .then_inc(sb_weights, 1)
                if j % 4 == 3 and j >= 7:
                    sb_save(act, j // 4 - 1)
            sb_save(act, 7)
            for name, t0, l0 in (("oa", 8, 0), ("ob", 20, 4)):
                sig, per = (out_saved, 2) if name == "oa" else (sb_saved, 2)
                if name == "ob":
                    act.wait_ge(act_ready, SPLIT0["w_out"] + 4)
                squares(name, lambda t: qkv[:, t0 + t, :], lambda t: (sig, per * (t + 1)))
                root(name)
                for t in range(4):
                    high("w_out", l0 + t)
            out_phase("w_out", "ffn0")
            root("ffn0")
            act.wait_ge(chunk_done, C0["up0"])
            for t in range(KT):
                high("up0", t, bias=modv(SHIFT_FFN, t))
            up(0)
            down(0, "final_g")
            root("final_g")
            squares("a1", lambda t: x[:, t, :], lambda t: (x_ready, X0["final_g"] + t + 1))
            root("a1")
            for t in range(KT):
                high("a_in", t)
            act.preload_act_table(ACT.Gelu_apprx_tanh)
            with act.Fori(0, 3) as i:
                for s in range(2):
                    split_loop(C0["a_in"] + 2, i, s)
                    act.wait_ge(group_free, G0["a_in"] + 2 * i + s + 1)
                    zt = z_a[:, bass.ds(4 * i + 2 * s, 2), :]
                    act.activation(zt, zt, ACT.Gelu_apprx_tanh).then_inc(gelu_done, 1)
            split_at(C0["a_out"])
            split_at(C0["a_out"] + 1)
            act.wait_ge(group_free, G0["a_out"])
            act.activation(z_a[:, 12:14, :], z_a[:, 12:14, :], ACT.Copy, scale=HD ** -0.5).then_inc(q_scaled, 1)
            for t in range(NT):
                act.wait_ge(tr_saved, TR0["v_a"] + 2 * t + 2)
                if t:
                    act.wait_ge(v_ss, t)
                act.activation(vsq_junk[:, :], vtok_a[:, t, :], ACT.Square,
                               accum_out=tok_ss[:, t:t + 1]).then_inc(v_ss, 1)
            act.wait_ge(v_ss, 4)
            act.activation(tok_rms, tok_ss, ACT.Sqrt, scale=1.0 / TOK, bias=eps).then_inc(v_root, 1)
            softmax("mem_a")
            direct(act, "a_out", oT_a)
            out_phase("a_out", "a2")
            root("a2")
            act.wait_ge(chunk_done, C0["up1"])
            for t in range(KT):
                high("up1", t)
            up(1)
            down(1, "b1")
            root("b1")
            for t in range(KT):
                high("kv", t)
            with act.Fori(0, 2) as i:
                for s in range(2):
                    split_loop(C0["kv"] + 2, i, s)
            for j in range(4):
                c = C0["kv"] + 6 + j
                split_at(c, KT * KV_TAIL[2 + j][1] if j < 2 else 2048)
            softplus(f_rows[:, 2, :], f_clamped, f_exped, f_logged, 1)
            act.wait_ge(chunk_done, C0["b_q"])
            for t in range(KT):
                high("b_q", t)
            with act.Fori(0, 2) as i:
                for s in range(2):
                    split_loop(C0["b_q"] + 2, i, s)
            act.wait_ge(group_free, G0["b_out"])
            act.activation(q_b[:, :, :], q_b[:, :, :], ACT.Copy, scale=HD ** -0.5).then_inc(q_scaled, 1)
            softmax("fox")
            softmax("mem_b")
            direct(act, "b_out", oT_b)
            out_phase("b_out", "b2")
            root("b2")
            act.wait_ge(chunk_done, C0["up2"])
            for t in range(KT):
                high("up2", t)
            up(2)
            down(2, "final")
            root("final")

        @block.vector
        def _(dve):
            def split_w(c, slot, n=2048):
                dve.wait_ge(w_hi_done, c + 1)
                dve.tensor_tensor(w_lo[slot][:, 0:n], w_stage[slot][:, 0:n],
                                  w_hi[slot][:, 0:n].bitcast(FP32), ALU.subtract).then_inc(w_ready, 1)

            def copy_group(c, tile0, slot, dst, n=SEQ):
                dve.wait_ge(tile0_done, tile0)
                dve.tensor_copy(dst(0), bank[2 * slot][:, 0:n])
                dve.wait_ge(chunk_done, c + 1)
                dve.tensor_copy(dst(1), bank[2 * slot + 1][:, 0:n]).then_inc(group_free, 1)

            def add_squares(name, t):
                dve.wait_ge(sq_ready, SQ0[name] + t + 1)
                if t > 1:
                    dve.wait_ge(sq_added, ADD0[name] + t - 1)
                dve.tensor_tensor(sq_sum[:, :], sq_sum[:, :], sq[:, t % 2, :], ALU.add)\
                    .then_inc(sq_added, 1)

            def invert(name):
                n = NORM[name]
                dve.wait_ge(root_ready, n + 1)
                dve.reciprocal(rms[:, :], rms[:, :]).then_inc(rms_ready, 1)
                dve.wait_ge(rms_ready, n + 1)

            def scale_tiles(ph, tiles, src, col, bias=None):
                def low(t):
                    dve.wait_ge(act_hi_done, SPLIT0[ph] + t + 1)
                    hi = act_hi[:, t, :].bitcast(FP32)
                    if bias is None:
                        dve.tensor_tensor(act_lo[:, t, :], tmp[:, t % 4, :], hi, ALU.subtract)\
                            .then_inc(act_ready, 1)
                    else:
                        dve.scalar_tensor_tensor(out=act_lo[:, t, :], in0=tmp[:, t % 4, :],
                                                 scalar=bias(t), in1=hi, op0=ALU.add,
                                                 op1=ALU.subtract).then_inc(act_ready, 1)
                for n, t in enumerate(tiles):
                    dve.scalar_tensor_tensor(out=tmp[:, t % 4, :], in0=src(t), scalar=col(t),
                                             in1=rms[:, :], op0=ALU.mult, op1=ALU.mult)\
                        .then_inc(scaled, 1)
                    if n:
                        low(t - 1)
                low(tiles[-1])

            def direct(ph, src):
                for t in range(KT):
                    dve.wait_ge(act_hi_done, SPLIT0[ph] + t + 1)
                    dve.tensor_tensor(act_lo[:, t, :], src[:, t, :], act_hi[:, t, :].bitcast(FP32),
                                      ALU.subtract).then_inc(act_ready, 1)

            def tr_bank(name, b):
                n = TR0[name] + b
                dve.wait_ge(tr_ready, n + 1)
                return bank[6 + n % 2]

            def shift_scores(h, i):
                j = 4 * h["head"] + i
                n = h["keys"][i]
                dve.wait_ge(scores_ready, j + 1)
                if j >= 4:
                    dve.wait_ge(probs_ready, j - 3)
                dve.tensor_tensor_reduce(out=tmp[:, j % 4, 0:n], in0=bank[2 + j % 4][:, 0:n],
                                         in1=h["bias"](i), scale=-1.0, scalar=3.0e38, op0=ALU.add,
                                         op1=ALU.min, accum_out=neg_max[:, j % 8:j % 8 + 1])\
                    .then_inc(scores_read, 1)

            def normalize(h, i):
                j = 4 * h["head"] + i
                n = h["keys"][i]
                dve.wait_ge(probs_ready, j + 1)
                inv = row_inv[:, j % 8:j % 8 + 1]
                dve.reciprocal(inv, row_sum[:, j % 8:j % 8 + 1]).then_inc(inv_ready, 1)
                dve.wait_ge(inv_ready, j + 1)
                p = probs[:, h["head"] % 2, i, 0:n]
                dve.tensor_scalar(p, p, inv, None, ALU.mult).then_inc(probs_normed, 1)

            def softmax(name):
                for h in session(name):
                    for i in range(4):
                        shift_scores(h, i)
                        if i:
                            normalize(h, i - 1)
                    normalize(h, 3)

            def ada(n, part, k, load_count):
                dve.wait_ge(ada_loaded[n], load_count)
                acc = ada_acc[:, part * 2048:(part + 1) * 2048]
                dve.scalar_tensor_tensor(out=acc, in0=ada_stage[n][:, :], scalar=k, in1=acc,
                                         op0=ALU.mult, op1=ALU.add).then_inc(ada_added, 1)

            def mod_columns(lo, hi, n, scale):
                dve.wait_ge(mod_summed, n)
                dve.tensor_tensor(mod[:, lo:hi], bank[5][:, lo:hi], vec[:, P + lo:P + hi], ALU.add)\
                    .then_inc(mod_added, 1)
                dve.wait_ge(mod_added, n)
                dve.tensor_scalar(mod[:, 8 * scale:8 * scale + 8], mod[:, 8 * scale:8 * scale + 8],
                                  1.0, None, ALU.add).then_inc(mod_ready, 1)
                dve.wait_ge(mod_ready, n)

            def up(f):
                c0, g0, n0 = C0[f"up{f}"], G0[f"up{f}"], FT // 2 * f
                va = P * (2 + 2 * f)
                with dve.Fori(0, FT // 2) as i:
                    for s in range(2):
                        split_w(2 * i + s + c0 + 2, s)
                        for m in range(2):
                            n = 2 * s + m
                            t, b = tmp[:, n, :], bank[n]
                            w0 = vec[:, bass.ds(2 * i + va + FT * s + m, 1)]
                            w1 = vec[:, bass.ds(2 * i + va + CT + FT * s + m, 1)]
                            dve.wait_ge(tap_started, 4 * i + 4 * n0 + n + 1)
                            dve.scalar_tensor_tensor(out=t[:, 1:SEQ], in0=b[:, 0:SEQ - 1], scalar=w1,
                                                     in1=t[:, 1:SEQ], op0=ALU.mult, op1=ALU.add)\
                                .then_inc(tap_added, 1)
                            dve.wait_ge(tap_added, 4 * i + 4 * n0 + n + 1)
                            dve.scalar_tensor_tensor(out=t[:, 2:SEQ], in0=b[:, 0:SEQ - 2], scalar=w0,
                                                     in1=t[:, 2:SEQ], op0=ALU.mult, op1=ALU.add)\
                                .then_inc(group_free if m else taps_done, 1)
                    for m in range(2):
                        dve.wait_ge(gate_done, 2 * i + 2 * n0 + m + 1)
                        if m == 0:
                            dve.wait_ge(taps_done, 2 * i + 2 * n0 + 2)
                        else:
                            dve.wait_ge(group_free, 2 * i + g0 + 2)
                        dve.tensor_tensor(tmp[:, m, :], tmp[:, m, :], tmp[:, 2 + m, :], ALU.mult)\
                            .then_inc(mid_done, 1)
                    for m in range(2):
                        dve.wait_ge(mid_hi_done, 2 * i + 2 * n0 + m + 1)
                        dve.tensor_tensor(mid_lo[:, bass.ds(2 * i + m, 1), :], tmp[:, m, :],
                                          mid_hi[:, bass.ds(2 * i + m, 1), :].bitcast(FP32),
                                          ALU.subtract).then_inc(mid_ready, 1)

            def update(ph, g, c, gate):
                for m in range(2):
                    t = 2 * g + m
                    if m == 0:
                        dve.wait_ge(tile0_done, first_tiles(G0[ph] + g))
                    else:
                        dve.wait_ge(chunk_done, c + 1)
                    b = bank[2 * (g % 2) + m][:, :]
                    if gate is None:
                        last = dve.tensor_tensor(x[:, t, :], b, x[:, t, :], ALU.add)
                    else:
                        last = dve.scalar_tensor_tensor(out=x[:, t, :], in0=b, scalar=modv(gate, t),
                                                        in1=x[:, t, :], op0=ALU.mult, op1=ALU.add)
                    last.then_inc(group_free if m else x_ready, 1)

            def out_phase(ph, name, gate=None):
                for g in range(4):
                    update(ph, g, C0[ph] + g, gate)
                    for t in range(max(1, 2 * g - 2), 2 * g):
                        add_squares(name, t)
                    if g < 3:
                        split_w(C0[ph] + g + 2, g % 2)
                add_squares(name, 6)
                add_squares(name, 7)
                split_w(C0[ph] + 5, 1)
                invert(name)

            def down(f, name, gate=None):
                def split_next(n):
                    if C0[f"down{f}"] + n < N_CHUNKS:
                        split_w(C0[f"down{f}"] + n, n % 2,
                                6 * CHUNK_COLS if n % 3 == 2 and n < 12 else 2048)
                for g in range(4):
                    for r in range(2):
                        split_next(3 * g + r + 2)
                    update(f"down{f}", g, C0[f"down{f}"] + 3 * g + 2, gate)
                    for t in range(max(1, 2 * g - 2), 2 * g):
                        add_squares(name, t)
                    if g < 3:
                        split_next(3 * g + 4)
                add_squares(name, 6)
                add_squares(name, 7)
                split_next(13)
                invert(name)

            dve.wait_ge(mem_root, 1)
            dve.reciprocal(tok_rms[:, 0:2], tok_rms[:, 0:2]).then_inc(mem_rms, 1)
            dve.wait_ge(mem_rms, 1)
            for t in range(2):
                dve.tensor_scalar(mem_tok[:, t, :], mem_tok[:, t, :], tok_rms[:, t:t + 1], None,
                                  ALU.mult).then_inc(mem_normed, 1)
            sizes = [N_VEC, 48] + [2 * CT] * 6
            for b in range(2):
                src = tr_bank("vec", b)
                for i in range(4 * b, 4 * b + 4):
                    last = dve.tensor_copy(vec[:, P * i:P * i + sizes[i]],
                                           src[:, P * (i % 4):P * (i % 4) + sizes[i]])
                last.then_inc(tr_saved, 1)
            split_w(0, 0)
            split_w(1, 1)
            dve.wait_ge(tr_saved, TR0["vec"] + 2)
            for k in range(KT):
                src = tr_bank("mem", k)
                for l, name in enumerate(("a_mem_norm_2", "b_mem_norm_2")):
                    last = dve.tensor_scalar(mem_scaled[:, l, k, :], src[:, 0:NMEM], gain(name, k),
                                             None, ALU.mult)
                last.then_inc(tr_saved, 1)
            for k in range(KT):
                dve.tensor_copy(x[:, k, :], tr_bank("x", k)[:, :]).then_inc(tr_saved, 1)
            for l in range(2):
                dve.wait_ge(mem_hi_done, l + 1)
                dve.tensor_tensor(mem_lo[:, l, :, :], mem_scaled[:, l, :, :],
                                  mem_hi[:, l, :, :].bitcast(FP32), ALU.subtract).then_inc(mem_split, 1)
            dve.wait_ge(rb_loaded, 16)
            dve.tensor_copy(rel_rows[:, 0:384], rb_rows[:, RB - 1:RB].to_broadcast([8, 384]))\
                .then_inc(rel_flat, 1)
            dve.tensor_copy(rel_rows[:, 384:RROW - 1], rb_rows[:, RB - 2:0:-1]).then_inc(rel_flat, 1)
            dve.memset(rel_rows[:, RROW - 1:RROW], 0.0).then_inc(rel_flat, 1)
            for t in range(1, KT):
                add_squares("mix", t)
            dve.wait_ge(c_act, 1)
            dve.wait_ge(consts_set, 14)
            mem_dst = [kmT_a[:, :, :], vmT[:, 0, :, :], kmT_b0[:, :, :], vmT[:, 1, :, :]]
            for c in range(4):
                split_w(c + 2, c % 2)
                copy_group(c, first_tiles(c), c % 2, lambda m: mem_dst[c][:, m, :], n=NMEM)
                for k in (2 * c, 2 * c + 1):
                    if k:
                        dve.wait_ge(ada_added, k)
                    ada(k % 2, 0, sig_c[:, k:k + 1], 16 * (k // 2 + 1))
            for name, dst in (("vm_a", vm_a), ("vm_b", vm_b0)):
                dve.tensor_copy(dst[:, :, :].rearrange("p a b -> p (a b)"), tr_bank(name, 0)[:, :])\
                    .then_inc(tr_saved, 1)
            invert("mix")
            mod_columns(0, 16, 1, SCALE_MIX)
            scale_tiles("w_in", range(KT), lambda t: x[:, t, :], lambda t: modv(SCALE_MIX, t),
                        bias=lambda t: modv(SHIFT_MIX, t))
            for k in (0, 1):
                for s in range(2):
                    dve.wait_ge(ada_added, 2 * k + s + 7)
                    ada(s, 1 + s, sig_c[:, k:k + 1], 16 * (k + 5))
            with dve.Fori(0, 6) as i:
                for s in range(2):
                    split_w(2 * i + s + C0["w_in"] + 2, s)
                    copy_group(2 * i + s + C0["w_in"], 2 * i + s + first_tiles(G0["w_in"]), s,
                               lambda m: qkv[:, bass.ds(4 * i + 2 * s + m, 1), :])
                    dve.wait_ge(ada_added, 2 * i + s + 11)
                    ada(s, 1 + s, stats[:, bass.ds(i + 38, 1)], 16 * i + 112)
            mod_columns(16, 48, 2, SCALE_FFN)
            for b in range(8):
                half, t = b // 4, b % 4
                dve.tensor_copy(v_tok[:, t, 512 * half:512 * half + 512], tr_bank("v_l0", b)[:, :])\
                    .then_inc(tr_saved, 1)
            dve.wait_ge(rel_back, 16)
            dve.memset(rel[0:HD, :, SEQ - HD:SEQ], NEG).then_inc(rel_masked, 1)
            dve.wait_ge(rel_masked, 1)
            softmax("rel")
            for j in range(SB_STEPS + 1):
                if j < SB_STEPS:
                    n, r, kj, q0 = sb_step(j)
                    dve.wait_ge(sb_scores, j + 1)
                    dve.tensor_scalar(tmp[:, j % 4, q0:SEQ], bank[2 + j % 6][:, q0:SEQ], CLAMP, None,
                                      ALU.min).then_inc(sb_clamped, 1)
                if j >= 1:
                    i = j - 1
                    n, r, kj, q0 = sb_step(i)
                    dve.wait_ge(sb_logged, i + 1)
                    if n >= 2 and r == 0:
                        dve.wait_ge(sb_tail, 4 * (n - 1))
                    dve.tensor_tensor(probs[:, n % 2, r, q0:SEQ], bank[2 + i % 6][:, q0:SEQ],
                                      tmp[:, i % 4, q0:SEQ], ALU.max).then_inc(sb_plus, 1)
            for name, t0, l0, g in (("oa", 8, 0, "g_a"), ("ob", 20, 4, "g_b")):
                for t in range(1, 4):
                    add_squares(name, t)
                invert(name)
                scale_tiles("w_out", range(l0, l0 + 4), lambda t: qkv[:, t0 + t - l0, :],
                            lambda t: gain(g, t - l0))
            out_phase("w_out", "ffn0", GATE_MIX)
            scale_tiles("up0", range(KT), lambda t: x[:, t, :], lambda t: modv(SCALE_FFN, t),
                        bias=lambda t: modv(SHIFT_FFN, t))
            up(0)
            down(0, "final_g", GATE_FFN)
            for t in range(KT):
                dve.scalar_tensor_tensor(out=x[:, t, :], in0=x[:, t, :], scalar=gain("final_g", t),
                                         in1=rms[:, :], op0=ALU.mult, op1=ALU.mult).then_inc(x_ready, 1)
            for t in range(1, KT):
                add_squares("a1", t)
            invert("a1")
            scale_tiles("a_in", range(KT), lambda t: x[:, t, :], lambda t: gain("a_norm1_2", t))
            with dve.Fori(0, 3) as i:
                for s in range(2):
                    split_w(2 * i + s + C0["a_in"] + 2, s)
                    copy_group(2 * i + s + C0["a_in"], 2 * i + s + first_tiles(G0["a_in"]), s,
                               lambda m: z_a[:, bass.ds(4 * i + 2 * s + m, 1), :])
            for j in range(2):
                split_w(C0["a_out"] + j, j)
                dve.wait_ge(chunk_done, C0["a_in"] + 7 + j)
                dve.tensor_copy(z_a[:, 12 + j, :], bank[2 * j][:, :]).then_inc(group_free, 1)
            dve.tensor_tensor(wsT[:, :, :], tr_bank("ws", 0)[:, :].rearrange("p (g t) -> p g t", t=P),
                              tri[:, :].rearrange("p (o t) -> p o t", o=1).to_broadcast([P, GROUPS, P]),
                              ALU.mult).then_inc(tr_saved, 1)
            dve.memset(zero_bias[:, :], 0.0).then_inc(zero_set, 1)
            for b in range(8):
                t, half = b // 2, b % 2
                dve.tensor_copy(vtok_a[:, t, 384 * half:384 * (half + 1)], tr_bank("v_a", b)[:, 0:384])\
                    .then_inc(tr_saved, 1)
            dve.wait_ge(v_root, 1)
            dve.reciprocal(tok_rms, tok_rms).then_inc(v_rms, 1)
            dve.wait_ge(v_rms, 1)
            for t in range(NT):
                dve.tensor_scalar(vtok_a[:, t, :], vtok_a[:, t, :], tok_rms[:, t:t + 1], None,
                                  ALU.mult).then_inc(v_normed, 1)
            for ct in range(6):
                dve.wait_ge(gm_ready, ct + 1)
                for lo, hi, g in gm_parts(ct):
                    dve.scalar_tensor_tensor(
                        out=oT_a[lo:hi, ct, :].rearrange("p (n t) -> p n t", t=P),
                        in0=bank[ct % 4][lo:hi, :].rearrange("p (n t) -> p n t", t=P),
                        scalar=vec[lo:hi, VEC0["a_v_norm_2"] + ct:VEC0["a_v_norm_2"] + ct + 1],
                        in1=bs[lo:hi, g, :].rearrange("p (o t) -> p o t", o=1)
                        .to_broadcast([hi - lo, NT, P]), op0=ALU.mult, op1=ALU.add).then_inc(gm_biased, 1)
                dve.wait_ge(gm_biased, gm_count(ct))
                dve.tensor_tensor(oT_a[:, ct, :], oT_a[:, ct, :], z_a[:, ct, :], ALU.mult)\
                    .then_inc(gm_done, 1)
            dve.wait_ge(zero_set, 1)
            softmax("mem_a")
            direct("a_out", oT_a)
            out_phase("a_out", "a2")
            scale_tiles("up1", range(KT), lambda t: x[:, t, :], lambda t: gain("a_norm2_2", t))
            up(1)
            down(1, "b1")
            scale_tiles("kv", range(KT), lambda t: x[:, t, :], lambda t: gain("kv_norm_2", t))
            with dve.Fori(0, 2) as i:
                for s in range(2):
                    split_w(2 * i + s + C0["kv"] + 2, s)
                    copy_group(2 * i + s + C0["kv"], 2 * i + s + first_tiles(G0["kv"]), s,
                               lambda m: kv_b[:, bass.ds(4 * i + 2 * s + m, 1), :])
            dve.wait_ge(bf_loaded, 16)
            for j in range(4):
                c = C0["kv"] + 4 + j
                split_w(c + 2, j % 2, KT * KV_TAIL[2 + j][1] if j < 2 else 2048)
                if j == 0:
                    copy_group(c, first_tiles(G0["kv"] + 4), 0, lambda m: kv_b[:, 8 + m, :])
                elif j < 3:
                    dve.wait_ge(chunk_done, c + 1)
                    dve.tensor_copy(kv_b[:, 9 + j, :], bank[2 * (j % 2)][:, :]).then_inc(group_free, 1)
                else:
                    dve.wait_ge(chunk_done, c + 1)
                    dve.tensor_scalar(f_rows[:, 0, :], bank[2][0:FOX, :], b_f, -1.0, ALU.add, ALU.mult)\
                        .then_inc(group_free, 1)
            dve.wait_ge(group_free, G0["b_q"])
            dve.tensor_scalar(f_rows[:, 2, :], f_rows[:, 0, :], CLAMP, None, ALU.min).then_inc(f_clamped, 1)
            dve.memset(triext[:, P:SEQ], 1.0).then_inc(tri_set, 1)
            dve.tensor_copy(triext[:, 0:P], tri[:, :]).then_inc(tri_set, 1)
            dve.memset(zero_bias[:, :], 0.0).then_inc(zero_set, 1)
            for b in range(8):
                t, half = b // 2, b % 2
                dve.tensor_copy(vtok_b[:, t, 384 * half:384 * (half + 1)], tr_bank("v_b", b)[:, 0:384])\
                    .then_inc(tr_saved, 1)
            dve.wait_ge(f_logged, 1)
            dve.tensor_tensor(f_rows[:, 1, :], f_rows[:, 2, :], f_rows[:, 0, :], ALU.max).then_inc(f_plus, 1)
            dve.tensor_copy(lfT, tr_bank("f", 0)[:, 0:NT * FOX].rearrange("p (t f) -> p t f", f=FOX))\
                .then_inc(tr_saved, 1)
            dve.wait_ge(f_summed, 1)
            dve.tensor_copy(decay[0:FOX, 0, :], bank[4][0:FOX, :]).then_inc(f_saved, 1)
            scale_tiles("b_q", range(KT), lambda t: x[:, t, :], lambda t: gain("b_norm1_2", t))
            with dve.Fori(0, 2) as i:
                for s in range(2):
                    split_w(2 * i + s + C0["b_q"] + 2, s)
                    copy_group(2 * i + s + C0["b_q"], 2 * i + s + first_tiles(G0["b_q"]), s,
                               lambda m: q_b[:, bass.ds(4 * i + 2 * s + m, 1), :])
            dve.wait_ge(decay_back, 16)
            softmax("fox")
            dve.wait_ge(zero_set, 2)
            softmax("mem_b")
            direct("b_out", oT_b)
            out_phase("b_out", "b2")
            scale_tiles("up2", range(KT), lambda t: x[:, t, :], lambda t: gain("b_norm2_2", t))
            up(2)
            down(2, "final")
            for t in range(KT):
                dve.scalar_tensor_tensor(out=y[:, t, :], in0=x[:, t, :], scalar=gain("final_norm_2", t),
                                         in1=rms[:, :], op0=ALU.mult, op1=ALU.mult).then_inc(y_ready, 1)
            for b in range(8):
                t, half = b // 2, b % 2
                dve.tensor_copy(y_tok[:, t, 512 * half:512 * (half + 1)], tr_bank("out", b)[:, :])\
                    .then_inc(tr_saved, 1)


INPUTS = ["x", "c", "w_ada", "b_ada", "w_in", "rel_bias", "g_a", "g_b", "w_out", "w_up", "conv_w",
          "conv_b", "w_down", "final_g", "mem_2", "a_norm1_2", "a_w_in_2", "a_v_norm_2", "a_w_s_2",
          "a_b_s_2", "a_mem_norm_2", "a_w_mem_kv_2", "a_w_out_2", "a_norm2_2", "a_ffn_in_2",
          "a_ffn_conv_2", "a_ffn_conv_b_2", "a_ffn_out_2", "kv_norm_2", "w_kv_2", "b_f_2",
          "b_norm1_2", "b_w_q_2", "b_mem_norm_2", "b_w_mem_kv_2", "b_w_out_2", "b_norm2_2",
          "b_ffn_in_2", "b_ffn_conv_2", "b_ffn_conv_b_2", "b_ffn_out_2", "final_norm_2"]


def kernel(**inputs):
    import numpy as np
    import concourse.bacc as bacc
    from concourse.bass_utils import run_bass_kernel_spmd

    nc = bacc.Bacc("TRN2", target_bir_lowering=False, num_devices=1)
    arrays, aps = {}, {}
    for name in INPUTS:
        v = np.ascontiguousarray(inputs[name])
        arrays["in_" + name] = v
        aps[name] = nc.dram_tensor("in_" + name, v.shape, mybir.dt.from_np(v.dtype),
                                   kind="ExternalInput").ap()
    out = nc.dram_tensor("out_x", (1, SEQ, D), FP32, kind="ExternalOutput").ap()
    program(nc, aps, out)
    r = run_bass_kernel_spmd(nc, [arrays], core_ids=[0])
    return r.results[0]["out_x"]
```

```python
import concourse.bass as bass
from concourse import mybir
from contextlib import ExitStack

FP32 = mybir.dt.float32
FP32R = mybir.dt.float32r
ALU = mybir.AluOpType
ACT = mybir.ActivationFunctionType

P = 128
SEQ = 512
D = 1024
KT = D // P
NT = SEQ // P
HD = 64
DFF = 2816
FT = DFF // P
CT = 2 * FT
TOK = 768
NMEM = 256
GROUPS = 4
GW = TOK // GROUPS
FOX = TOK // HD
CHUNK_COLS = 256
NEG = -1e30
EPS = 1e-6
CLAMP = 40.0
RB = 257
RROW = 640

PHASES = [("mem_a", 2, 2), ("mem_b", 2, 2), ("w_in", 12, 12), ("w_out", 4, 4), ("up0", 22, 22),
          ("down0", 12, 4), ("a_in", 8, 8), ("a_out", 4, 4), ("up1", 22, 22), ("down1", 12, 4),
          ("b_q", 4, 4), ("kv", 8, 8), ("b_out", 4, 4), ("up2", 22, 22), ("down2", 12, 4)]
C0, G0 = {}, {}
_c = _g = 0
for _name, _nc, _ng in PHASES:
    C0[_name], G0[_name] = _c, _g
    _c, _g = _c + _nc, _g + _ng
N_CHUNKS = _c
ONE_TILE_GROUPS = [G0["a_in"] + 3, G0["a_in"] + 4, G0["kv"] + 5, G0["kv"] + 6, G0["kv"] + 7]


def first_tiles(g):
    return g + 1 - sum(x <= g for x in ONE_TILE_GROUPS)


NORMS = [("mix", 8), ("oa", 4), ("ob", 4), ("ffn0", 8), ("final_g", 8), ("a2", 8),
         ("b1", 8), ("b2", 8), ("final", 8)]
NORM = {name: i for i, (name, _) in enumerate(NORMS)}
SQ0 = {name: sum(n for _, n in NORMS[:i]) for i, (name, _) in enumerate(NORMS)}
ADD0 = {name: sum(n - 1 for _, n in NORMS[:i]) for i, (name, _) in enumerate(NORMS)}

X0 = {"w_out": 0, "down0": 4, "final_g": 8, "a_out": 16, "down1": 20, "b_out": 24, "down2": 28}
SPLIT0 = {n: 8 * i for i, n in enumerate(["w_in", "w_out", "up0"])}
GAIN0 = {n: 8 * i for i, n in enumerate(["a_in", "up1", "b_q", "kv", "up2"])}

VECTORS = [("c", 8), ("g_a", 4), ("g_b", 4), ("final_g", 8), ("a_norm1_2", 8), ("a_v_norm_2", 6),
           ("a_norm2_2", 8), ("kv_norm_2", 8), ("b_norm1_2", 8), ("b_norm2_2", 8),
           ("final_norm_2", 8), ("a_mem_norm_2", 8), ("b_mem_norm_2", 8)]
VEC0 = {name: sum(n for _, n in VECTORS[:i]) for i, (name, _) in enumerate(VECTORS)}
N_VEC = sum(n for _, n in VECTORS)
CONVS = [("conv_w", "conv_b"), ("a_ffn_conv_2", "a_ffn_conv_b_2"), ("b_ffn_conv_2", "b_ffn_conv_b_2")]

BATCHES = [("vec", 1), ("mem", 8), ("conv", 2), ("vm_a", 1), ("vm_b", 1), ("v_l0", 8), ("ws", 1),
           ("v_a", 8), ("v_b", 8), ("f", 1), ("out", 8)]
TR0 = {name: sum(n for _, n in BATCHES[:i]) for i, (name, _) in enumerate(BATCHES)}

SESSIONS = [("rel", 8, True), ("mem_a", 4, False), ("fox", 12, True), ("mem_b", 4, False)]
HEAD0 = {name: sum(n for _, n, _ in SESSIONS[:i]) for i, (name, _, _) in enumerate(SESSIONS)}
HEAD_TURNS = [4 if causal else 2 for _, n, causal in SESSIONS for _ in range(n)]
TURN0 = [sum(HEAD_TURNS[:i]) for i in range(len(HEAD_TURNS))]


def program(nc, a, out):
    ctx = ExitStack()
    with ctx:
        def at(name, shape, offset, dt=FP32):
            return nc.alloc_sbuf_tensor_at(name, shape, dt, offset=offset)

        def sem(name):
            return ctx.enter_context(nc.semaphore(name))

        KB = 1024
        base = -(-nc.sbuf_base // 32) * 32
        o_x, o_act, o_w, o_m = base, base + 16 * KB, base + 48 * KB, base + 96 * KB
        o_tmp = o_m + 88 * KB
        o_small = o_tmp + 8 * KB

        x = at("x_res", [P, KT, SEQ], o_x)
        act_hi = at("act_hi", [P, KT, SEQ], o_act, FP32R)
        act_lo = at("act_lo", [P, KT, SEQ], o_act + 16 * KB, FP32R)
        probs = at("probs", [P, 2, NT, SEQ], o_act)
        probsT = at("probsT", [P, 2, NT, SEQ], o_act + 16 * KB)
        vec_rows = at("vec_rows", [P, 8, P], o_act)
        sq_junk = at("sq_junk", [P, D], o_x)
        mem_scaled = at("mem_scaled", [P, 2, KT, NMEM], o_act + 8 * KB)

        w_stage = [at(f"w_stage{s}", [P, 2048], o_w + 8 * KB * s) for s in range(2)]
        w_hi = [at(f"w_hi{s}", [P, 2048], o_w + 8 * KB * (2 + s), FP32R) for s in range(2)]
        w_lo = [at(f"w_lo{s}", [P, 2048], o_w + 8 * KB * (4 + s), FP32R) for s in range(2)]

        mid_hi = at("mid_hi", [P, FT, SEQ], o_m, FP32R)
        mid_lo = at("mid_lo", [P, FT, SEQ], o_m + 44 * KB, FP32R)
        mid_val = at("mid_val", [P, FT, SEQ], o_m + 44 * KB)
        mem_hi = at("mem_hi", [P, 2, KT, NMEM], o_m, FP32R)
        mem_lo = at("mem_lo", [P, 2, KT, NMEM], o_m + 16 * KB, FP32R)
        x_tok = at("x_tok", [P, NT, D], o_m + 32 * KB)
        kmT_0 = at("kmT_0", [P, 2, 2, NMEM], o_m + 32 * KB)
        vm_0 = at("vm_0", [P, 2, 2, NMEM], o_m + 36 * KB)
        vmT = at("vmT", [P, 2, 2, NMEM], o_m + 40 * KB)
        qkv = at("qkv", [P, 24, SEQ], o_m)
        ada_acc = at("ada_acc", [P, 6144], o_m + 48 * KB)
        ada_stage = [at(f"ada_stage{s}", [P, 2048], o_m + (72 + 8 * s) * KB) for s in range(2)]
        rel = [at(f"rel{j}", [P, 4, SEQ], o_m + (48 + 24 * j) * KB) for j in range(2)]
        v_tok = at("v_tok", [P, NT, D], o_m + 56 * KB)
        z_a = at("z_a", [P, 14, SEQ], o_m)
        vtok_a = at("vtok_a", [P, NT, TOK], o_m + 28 * KB)
        ws_raw = at("ws_raw", [P, GROUPS, P], o_m + 40 * KB)
        wsT = at("wsT", [P, GROUPS, P], o_m + 42 * KB)
        bs = at("bs", [P, GROUPS, P], o_m + 44 * KB)
        o_hi_a = at("o_hi_a", [P, KT, SEQ], o_m + 48 * KB, FP32R)
        o_lo_a = at("o_lo_a", [P, KT, SEQ], o_m + 64 * KB, FP32R)
        vsq_junk = at("vsq_junk", [P, TOK], o_m + 80 * KB)
        zero_a = at("zero_a", [P, NMEM], o_m + 83 * KB)
        kmT_a = at("kmT_a", [P, 2, NMEM], o_m + 84 * KB)
        vm_a = at("vm_a", [P, 2, NMEM], o_m + 86 * KB)
        kv_b = at("kv_b", [P, 12, SEQ], o_m)
        o_hi_b = at("o_hi_b", [P, KT, SEQ], o_m + 12 * KB, FP32R)
        o_lo_b = at("o_lo_b", [P, KT, SEQ], o_m + 56 * KB, FP32R)
        kvm_hi = at("kvm_hi", [P, KT, SEQ], o_m + 44 * KB, FP32R)
        kvm_lo = at("kvm_lo", [P, KT, SEQ], o_m + 60 * KB, FP32R)
        q_b = at("q_b", [P, KT, SEQ], o_m + 28 * KB)
        vtok_b = at("vtok_b", [P, NT, TOK], o_m + 44 * KB)
        decay = at("decay", [P, FOX, SEQ], o_m + 56 * KB)
        kmT_b = at("kmT_b", [P, 2, NMEM], o_m + 80 * KB)
        vm_b = at("vm_b", [P, 2, NMEM], o_m + 82 * KB)
        triext = at("triext", [P, SEQ], o_m + 84 * KB)
        zero_b = at("zero_b", [P, NMEM], o_m + 86 * KB)
        o_hi_0 = [at(f"o_hi_0{j}", [P, 4, SEQ], o_m + 24 * KB * j, FP32R) for j in range(2)]
        o_lo_0 = [at(f"o_lo_0{j}", [P, 4, SEQ], o_m + (24 * j + 8) * KB, FP32R) for j in range(2)]
        y = at("y", [P, KT, SEQ], o_m)
        y_tok = at("y_tok", [P, NT, D], o_m + 16 * KB)

        tmp = at("tmp", [P, 4, SEQ], o_tmp)
        mem_tok = at("mem_tok", [P, 2, D], o_tmp)

        here = [o_small]

        def small(name, shape, dt=FP32):
            n = 4
            for s in shape[1:]:
                n *= s
            t = at(name, shape, here[0], dt)
            here[0] += -(-n // 32) * 32
            return t

        vec = small("vec", [P, 8 * P])
        ident = small("ident", [P, P])
        neg_ones = small("neg_ones", [P, P])
        neg_upper = small("neg_upper", [P, P])
        tri = small("tri", [P, P])
        strict_neg = small("strict_neg", [P, P])
        causal_neg = small("causal_neg", [P, P])
        sq_sum = small("sq_sum", [P, SEQ])
        rel_rows = at("rel_rows", [8, RROW], here[0])
        rb_rows = at("rb_rows", [8, RB], here[0] + 4 * RROW)
        sq_sum2 = small("sq_sum2", [P, SEQ])
        rms2 = small("rms2", [P, SEQ])
        rms = small("rms", [P, SEQ])
        mod = small("mod", [P, 48])
        stats = small("stats", [P, 64])
        neg_max, row_sum, row_inv = stats[:, 0:8], stats[:, 8:16], stats[:, 16:24]
        tok_ss, eps, one_col = stats[:, 24:28], stats[:, 28:29], stats[:, 29:30]
        tok_rms, b_f = stats[:, 30:34], stats[0:FOX, 34:35]
        sig_c, gain_a1 = stats[:, 36:44], stats[:, 44:52]
        sq = tmp[:, 2:4, :]

        def squares_of(name, t):
            return rel[1][:, t % 2, :] if name == "oa" else sq[:, t % 2, :]

        f_rows = tmp[0:FOX, :, :]
        lfT = tmp[:, 3, 0:NT * FOX].rearrange("p (t f) -> p t f", f=FOX)

        def gain(name, t):
            return vec[:, VEC0[name] + t:VEC0[name] + t + 1]

        def modv(section, t):
            return mod[:, 8 * section + t:8 * section + t + 1]

        SHIFT_MIX, SCALE_MIX, GATE_MIX, SHIFT_FFN, SCALE_FFN, GATE_FFN = range(6)

        bank = [ctx.enter_context(nc.psum_tensor(f"bank{i}", [P, SEQ], FP32)) for i in range(8)]

        rel_dram = nc.dram_tensor("rel_scratch", [8, P, RROW], FP32)
        decay_dram = nc.dram_tensor("decay_scratch", [FOX, SEQ], FP32)
        mem_dram = nc.dram_tensor("mem_scratch", [2, P, 4 * NMEM], FP32)

        consts_set = sem("consts_set")
        vec_loaded = sem("vec_loaded")
        conv_loaded = sem("conv_loaded")
        x_turned = sem("x_turned")
        x_saved = sem("x_saved")
        x_loaded = sem("x_loaded")
        mem_loaded = sem("mem_loaded")
        rb_loaded = sem("rb_loaded")
        w_loaded = [sem(f"w_loaded{s}") for s in range(2)]
        w_hi_done = sem("w_hi_done")
        w_ready = sem("w_ready")
        tile0_done = sem("tile0_done")
        chunk_done = sem("chunk_done")
        group_free = sem("group_free")
        act_ready = sem("act_ready")
        act_hi_done = sem("act_hi_done")
        scaled = sem("scaled")
        gain_hi = sem("gain_hi")
        gain_ready = sem("gain_ready")
        sq2_ready, sq2_added, sum2_ready = sem("sq2_ready"), sem("sq2_added"), sem("sum2_ready")
        rms_squared, mean2_ready, root2_ready, rms2_ready, rms12_ready = (
            sem("rms_squared"), sem("mean2_ready"), sem("root2_ready"), sem("rms2_ready"),
            sem("rms12_ready"))
        gain_a1_set = sem("gain_a1_set")
        x_ready = sem("x_ready")
        sq_ready = sem("sq_ready")
        sq_added = sem("sq_added")
        sum_ready = sem("sum_ready")
        root_ready = sem("root_ready")
        rms_ready = sem("rms_ready")
        tr_ready = sem("tr_ready")
        tr_saved = sem("tr_saved")
        ada_loaded = [sem(f"ada_loaded{s}") for s in range(2)]
        ada_added = sem("ada_added")
        c_act = sem("c_act")
        mod_summed, mod_added, mod_ready = sem("mod_summed"), sem("mod_added"), sem("mod_ready")
        mem_ss, mem_root, mem_rms = sem("mem_ss"), sem("mem_root"), sem("mem_rms")
        mem_normed, mem_hi_done, mem_split = sem("mem_normed"), sem("mem_hi_done"), sem("mem_split")
        mem_stored, mem_back = sem("mem_stored"), sem("mem_back")
        rel_flat, rel_stored, rel_back, rel_masked = (
            sem("rel_flat"), sem("rel_stored"), sem("rel_back"), sem("rel_masked"))
        q_scaled, zq_scaled = sem("q_scaled"), sem("zq_scaled")
        tap_started, tap_added, taps_done = sem("tap_started"), sem("tap_added"), sem("taps_done")
        up_scaled = sem("up_scaled")
        gate_done, mid_done, mid_hi_done, mid_ready = (
            sem("gate_done"), sem("mid_done"), sem("mid_hi_done"), sem("mid_ready"))
        scores_ready, scores_read, probs_ready, inv_ready, probs_normed = (
            sem("scores_ready"), sem("scores_read"), sem("probs_ready"), sem("inv_ready"),
            sem("probs_normed"))
        pT_ready, pT_saved, out_ready, out_saved, out_low = (
            sem("pT_ready"), sem("pT_saved"), sem("out_ready"), sem("out_saved"), sem("out_low"))
        sb_scores, sb_clamped, sb_exped, sb_logged, sb_plus = (
            sem("sb_scores"), sem("sb_clamped"), sem("sb_exped"), sem("sb_logged"), sem("sb_plus"))
        sb_tail, sb_weights, sb_out, sb_saved = (
            sem("sb_tail"), sem("sb_weights"), sem("sb_out"), sem("sb_saved"))
        gelu_done, gm_loaded, v_ss, v_root, v_rms, v_normed = (
            sem("gelu_done"), sem("gm_loaded"), sem("v_ss"), sem("v_root"), sem("v_rms"),
            sem("v_normed"))
        gm_ready, gm_biased, gm_done, gm_hi, gm_split, zero_set = (
            sem("gm_ready"), sem("gm_biased"), sem("gm_done"), sem("gm_hi"), sem("gm_split"),
            sem("zero_set"))
        f_neg, f_clamped, f_exped, f_logged, f_plus, f_summed, f_saved = (
            sem("f_neg"), sem("f_clamped"), sem("f_exped"), sem("f_logged"), sem("f_plus"),
            sem("f_summed"), sem("f_saved"))
        tri_set, bf_loaded, decay_stored, decay_back = (
            sem("tri_set"), sem("bf_loaded"), sem("decay_stored"), sem("decay_back"))
        y_ready, out_stored = sem("y_ready"), sem("out_stored")

        def rows(name):
            w = a[name]
            w = w[0] if len(w.shape) == 3 else w
            return w.rearrange("(k p) n -> p k n", p=P)

        UP = ["w_up", "a_ffn_in_2", "b_ffn_in_2"]
        DOWN = ["w_down", "a_ffn_out_2", "b_ffn_out_2"]
        A_IN = [(768, 256, [6, 7]), (1024, 256, [8, 9]), (1280, 256, [10, 11]), (1536, 128, [12]),
                (1664, 128, [13]), (0, 256, [0, 1]), (256, 256, [2, 3]), (512, 256, [4, 5])]
        KV_TAIL = [(1024, 256), (1280, 128), (1408, 128), (1536, FOX)]

        def w_part(t, nk, ncol):
            return t[:, 0:nk * ncol].rearrange("p (k n) -> p k n", n=ncol)

        def load_vectors(engine, vectors):
            for name, n in vectors:
                src = a[name].rearrange("o (k p) -> (o k) p", p=P) if len(a[name].shape) == 2 else \
                    a[name].rearrange("(k p) -> k p", p=P)
                engine.dma_start(vec_rows[VEC0[name]:VEC0[name] + n, 0, :], src).then_inc(vec_loaded, 16)

        nc_block = ctx.enter_context(nc.Block())
        block = nc_block

        @block.sync
        def _(sp):
            def load(c, src, nk, ncol, slot):
                if not isinstance(c, int) or c >= 2:
                    sp.wait_ge(w_ready, c - 1)
                sp.dma_start(w_part(w_stage[slot], nk, ncol), src).then_inc(w_loaded[slot], 16)

            def cols(w, k0, k1, n0, n=CHUNK_COLS):
                return w[:, k0:k1, bass.ds(n0, n)]

            def small_loads():
                for f, (w, b) in enumerate(CONVS):
                    for j in range(3):
                        sp.dma_start(vec_rows[CT * (j % 2):CT * (j % 2) + CT, 2 + 2 * f + j // 2, :],
                                     a[w][0, j, :].rearrange("(k p) -> k p", p=P))\
                            .then_inc(conv_loaded, 16)
                    sp.dma_start(vec_rows[CT:2 * CT, 3 + 2 * f, :],
                                 a[b].rearrange("o (k p) -> (o k) p", p=P)).then_inc(conv_loaded, 16)
                sp.dma_start(rb_rows[:, :], a["rel_bias"][0]).then_inc(rb_loaded, 16)
                sp.dma_start(b_f, a["b_f_2"].rearrange("(f o) -> f o", o=1)).then_inc(bf_loaded, 16)

            sp.dma_start(mem_tok[:, :, :], a["mem_2"][0].rearrange("(t p) d -> p t d", p=P))\
                .then_inc(mem_loaded, 16)
            load_vectors(sp, VECTORS[0::2])
            sp.dma_start(x_tok[:, :, :], a["x"][0].rearrange("(t p) d -> p t d", p=P))\
                .then_inc(x_loaded, 16)
            for ph, w in (("mem_a", rows("a_w_mem_kv_2")), ("mem_b", rows("b_w_mem_kv_2"))):
                if ph == "mem_b":
                    small_loads()
                for s in range(2):
                    load(C0[ph] + s, cols(w, 0, KT, CHUNK_COLS * s), KT, CHUNK_COLS, s)

            def stream(ph, w, pairs):
                with sp.Fori(0, pairs) as i:
                    for s in range(2):
                        load(C0[ph] + 2 * i + s, cols(w, 0, KT, 2 * CHUNK_COLS * i + CHUNK_COLS * s),
                             KT, CHUNK_COLS, s)

            def stream_up(f):
                w = rows(UP[f])
                with sp.Fori(0, FT // 2) as i:
                    for s in range(2):
                        load(C0[f"up{f}"] + 2 * i + s, cols(w, 0, KT, CHUNK_COLS * i + DFF * s),
                             KT, CHUNK_COLS, s)

            def stream_down(f):
                w = rows(DOWN[f])
                with sp.Fori(0, 2) as i:
                    for j in range(6):
                        k0 = 8 * (j % 3)
                        k1 = min(k0 + 8, FT)
                        load(C0[f"down{f}"] + 6 * i + j,
                             cols(w, k0, k1, 2 * CHUNK_COLS * i + CHUNK_COLS * (j // 3)),
                             k1 - k0, CHUNK_COLS, j % 2)

            def tail(ph, w, done, parts):
                for j, (n0, n) in enumerate(parts):
                    load(C0[ph] + done + j, w[:, :, n0:n0 + n], KT, n, j % 2)

            stream("w_in", rows("w_in"), 6)
            stream("w_out", rows("w_out"), 2)
            stream_up(0)
            stream_down(0)
            tail("a_in", rows("a_w_in_2"), 0, [(n0, n) for n0, n, _ in A_IN])
            stream("a_out", rows("a_w_out_2"), 2)
            stream_up(1)
            stream_down(1)
            stream("b_q", rows("b_w_q_2"), 2)
            stream("kv", rows("w_kv_2"), 2)
            tail("kv", rows("w_kv_2"), 4, KV_TAIL)
            stream("b_out", rows("b_w_out_2"), 2)
            stream_up(2)
            stream_down(2)
            for t in range(NT):
                sp.wait_ge(tr_saved, TR0["out"] + 2 * t + 2)
                sp.dma_start(out[0, P * t:P * (t + 1), :], y_tok[:, t, :]).then_inc(out_stored, 16)
            sp.wait_ge(out_stored, 16 * NT)

        @block.gpsimd
        def _(pool):
            def ada(n, src):
                if n >= 2:
                    pool.wait_ge(ada_added, n - 1)
                pool.dma_start(ada_stage[n % 2][:, :], src).then_inc(ada_loaded[n % 2], 16)

            w_ada = a["w_ada"][0]
            for k in range(2):
                ada(k, w_ada[P * k:P * (k + 1), 0:2048])
            ones = [(ident, 0.0), (neg_upper, -1.0), (tri, 1.0), (strict_neg, 0.0), (causal_neg, 0.0)]
            for t, v in ones:
                pool.memset(t[:, :], v).then_inc(consts_set, 1)
            pool.memset(neg_ones[:, :], -1.0).then_inc(consts_set, 1)
            pool.memset(eps, EPS).then_inc(consts_set, 1)
            pool.memset(one_col, 1.0).then_inc(consts_set, 1)
            pool.wait_ge(consts_set, 8)
            for t, op, fill, first, step, mult in (
                    (ident, ALU.not_equal, 1.0, 0, -1, 1),
                    (neg_upper, ALU.is_ge, 0.0, 0, -1, 1),
                    (tri, ALU.is_ge, 0.0, 0, 1, -1),
                    (strict_neg, ALU.is_ge, NEG, -1, 1, -1),
                    (causal_neg, ALU.is_ge, NEG, 0, -1, 1)):
                pool.affine_select(out=t[:, :], in_=t[:, :], compare_op=op, fill=fill, base=first,
                                   pattern=[[step, P]], channel_multiplier=mult).then_inc(consts_set, 1)
            for k in range(2, KT):
                ada(k, w_ada[P * k:P * (k + 1), 0:2048])

            pool.wait_ge(group_free, G0["mem_b"] + 1)
            pool.wait_ge(tr_saved, TR0["vm_b"] + 1)
            for n, t in enumerate((kmT_0, vm_0)):
                pool.dma_start(mem_dram.ap()[n], t[:, :, :, :].rearrange("p l a b -> p (l a b)"))\
                    .then_inc(mem_stored, 16)

            pool.wait_ge(rel_flat, 3)
            pool.dma_start(rel_dram.ap(), rel_rows[:, :].rearrange("h (o z) -> h o z", o=1)
                           .to_broadcast([8, P, RROW])).then_inc(rel_stored, 16)

            def rel_load(j):
                pool.dma_start(rel[j][:, :, :],
                               bass.AP(tensor=rel_dram.ap().tensor, offset=P - 1 + 4 * j * P * RROW,
                                       ap=[[RROW - 1, P], [P * RROW, 4], [1, SEQ]]))\
                    .then_inc(rel_back, 16)

            for k in range(KT):
                for s in range(2):
                    ada(8 + 2 * k + s, w_ada[P * k:P * (k + 1), 2048 * (s + 1):2048 * (s + 2)])
                if k == 3:
                    pool.wait_ge(rel_stored, 16)
                    pool.wait_ge(mod_summed, 1)
                    rel_load(0)
            pool.wait_ge(ada_added, 3 * KT - 1)
            pool.wait_ge(rel_back, 16)
            rel_load(1)

            pool.wait_ge(chunk_done, C0["a_in"])
            pool.dma_start(ws_raw[:, :, :], a["a_w_s_2"][0].rearrange("g t s -> t g s")).then_inc(gm_loaded, 16)
            pool.dma_start(bs[:, :, :].rearrange("p g t -> p (g t)"),
                           a["a_b_s_2"][0].rearrange("g t -> (g t)").rearrange("(o n) -> o n", o=1)
                           .to_broadcast([P, GROUPS * P])).then_inc(gm_loaded, 16)

            def mem_load(l, km, vm):
                for n, t in enumerate((km, vm)):
                    pool.dma_start(t[:, :, :].rearrange("p a b -> p (a b)"),
                                   mem_dram.ap()[n, :, 2 * NMEM * l:2 * NMEM * (l + 1)])\
                        .then_inc(mem_back, 16)

            pool.wait_ge(mem_stored, 32)
            mem_load(0, kmT_a, vm_a)
            pool.wait_ge(mem_back, 32)
            pool.wait_ge(chunk_done, C0["b_q"])
            mem_load(1, kmT_b, vm_b)
            pool.wait_ge(f_saved, 1)
            pool.dma_start(decay_dram.ap(), f_rows[:, 0, :]).then_inc(decay_stored, 16)
            pool.wait_ge(decay_stored, 16)
            pool.wait_ge(chunk_done, C0["b_out"])
            pool.dma_start(decay[:, :, :], bass.AP(tensor=decay_dram.ap().tensor, offset=0,
                                                   ap=[[0, P], [SEQ, FOX], [1, SEQ]])).then_inc(decay_back, 16)

        def head_rows(t, n):
            return t[HD * (n % 2):HD * (n % 2) + HD, n // 2, :]

        def session(name):
            heads = []
            for n in range({s: m for s, m, _ in SESSIONS}[name]):
                if name == "rel":
                    h = dict(q=head_rows(qkv[:, 0:4, :], n), k=head_rows(qkv[:, 4:8, :], n),
                             v=lambda kj, n=n: v_tok[:, kj, HD * n:HD * (n + 1)],
                             bias=lambda qi, n=n: rel[n // 4][:, n % 4, SEQ - P * (qi + 1):SEQ],
                             out=head_rows(qkv[:, 8:12, :], n), low=None)
                elif name == "fox":
                    h = dict(q=head_rows(q_b, n), k=head_rows(kv_b[:, 0:6, :], n),
                             v=lambda kj, n=n: vtok_b[:, kj, HD * n:HD * (n + 1)],
                             bias=lambda qi, n=n: decay[:, n, 0:P * (qi + 1)],
                             out=head_rows(o_hi_b, n), low=head_rows(o_lo_b, n))
                else:
                    km, vm, zero, q, oh, ol = (
                        (kmT_a, vm_a, zero_a, z_a[:, 12:14, :], o_hi_a, o_lo_a)
                        if name == "mem_a" else
                        (kmT_b, vm_b, zero_b, q_b[:, 6:8, :], o_hi_b, o_lo_b))
                    h = dict(q=head_rows(q, n), k=head_rows(km, n),
                             v=lambda kj, n=n, vm=vm: vm[:, kj, HD * n:HD * (n + 1)],
                             bias=lambda qi, zero=zero: zero[:, :], out=head_rows(oh[:, 6:8, :], n),
                             low=head_rows(ol[:, 6:8, :], n))
                causal = name in ("rel", "fox")
                h.update(head=HEAD0[name] + n, turn=TURN0[HEAD0[name] + n],
                         causal=causal, mask=name == "fox", part=HD * (n % 2),
                         keys=[P * (qi + 1) if causal else NMEM for qi in range(NT)],
                         turns=4 if causal else 2)
                heads.append(h)
            return heads

        def pairs(heads):
            return list(zip(heads + [None], [None] + heads))

        def query0(h, kj):
            return P * kj if h["causal"] else 0

        SB_STEPS = 4 * 8

        def SB_BANK(j):
            return bank[(2, 3, 4, 6, 7)[j % 5]]

        def sb_step(j):
            n, r = j // 4, j % 4
            return n, r, 3 - r, P * (3 - r)

        def gm_parts(ct):
            cuts = sorted({0, P} | {GW * g - P * ct for g in range(GROUPS) if 0 < GW * g - P * ct < P})
            return [(lo, hi, (P * ct + lo) // GW) for lo, hi in zip(cuts, cuts[1:])]

        def gm_count(ct):
            return sum(len(gm_parts(t)) for t in range(ct + 1))

        def sb_save(act, n):
            act.wait_ge(sb_out, n + 1)
            part = HD * (n % 2)
            act.activation(head_rows(qkv[:, 20:24, :], n), bank[n % 2][part:part + HD, :], ACT.Copy)\
                .then_inc(sb_saved, 1)

        def conv_src(f, s, m):
            return tmp[:, 2 + m, :] if f else bank[2 * s + m]

        def conv_tile(f, i, s, m):
            if s == 0:
                return tmp[:, m, :]
            return tmp[:, 2 + m, :] if f == 0 else mid_val[:, bass.ds(2 * i + m, 1), :]

        def taps(f, i, s, m):
            n0 = FT // 2 * f
            if f == 0 and m:
                return group_free, 2 * i + s + G0["up0"] + 1
            if f == 0:
                return taps_done, 2 * i + s + 1
            return taps_done, 4 * i + 4 * n0 - FT + 2 * s + m + 1

        @block.tensor
        def _(pe):
            def chunk(c, slot, nk, ncol, moving, g=None, gslot=0, start=True, stop=True, n=SEQ,
                      k0=0, tile_wait=None, chunk_wait=None, between=None):
                pe.wait_ge(w_ready, c + 1)
                if start and (not isinstance(g, int) or g >= 2):
                    pe.wait_ge(group_free, g - 1)
                if chunk_wait:
                    pe.wait_ge(*chunk_wait)
                hi, lo = w_part(w_hi[slot], nk, ncol), w_part(w_lo[slot], nk, ncol)
                tiles = -(-ncol // P)
                for m in range(tiles):
                    w = min(P, ncol - P * m)
                    dst = bank[2 * gslot + m][0:w, 0:n]
                    for k in range(nk):
                        if tile_wait is not None and m == 0:
                            pe.wait_ge(*tile_wait(k))
                        mh, ml = moving(k0 + k)
                        wh, wl = hi[:, k, P * m:P * m + w], lo[:, k, P * m:P * m + w]
                        pe.matmul(dst, wh, mh, start=start and k == 0, stop=False)
                        pe.matmul(dst, wh, ml, start=False, stop=False)
                        last = pe.matmul(dst, wl, mh, start=False, stop=stop and k == nk - 1)
                    if m == 0 and tiles == 2 and stop:
                        last.then_inc(tile0_done, 1)
                    if m == 0 and between:
                        between()
                last.then_inc(chunk_done, 1)

            def act(k):
                return act_hi[:, k, :], act_lo[:, k, :]

            def o_0(k):
                return o_hi_0[k // 4][:, k % 4, :], o_lo_0[k // 4][:, k % 4, :]

            def mid(k):
                return mid_hi[:, k, :], mid_lo[:, k, :]

            def gemm_pairs(ph, n, moving, tile_wait, between=None):
                def pair(i, first=None):
                    for s in range(2):
                        chunk(2 * i + C0[ph] + s, s, KT, CHUNK_COLS, moving, g=2 * i + G0[ph] + s,
                              gslot=s, tile_wait=tile_wait, between=first if s == 0 else None)
                if between:
                    pair(0, between)
                with pe.Fori(1 if between else 0, n) as i:
                    pair(i)

            def normed(ph):
                return lambda k: (act_ready, SPLIT0[ph] + k + 1)

            def gained(ph):
                return lambda k: (gain_ready, GAIN0[ph] + k + 1)

            def gemm_down(f):
                with pe.Fori(0, 2) as i:
                    for j in range(6):
                        k0 = 8 * (j % 3)
                        k1 = min(k0 + 8, FT)
                        chunk(C0[f"down{f}"] + 6 * i + j, j % 2, k1 - k0, CHUNK_COLS, mid,
                              g=G0[f"down{f}"] + 2 * i + j // 3, gslot=j // 3, start=j % 3 == 0,
                              stop=j % 3 == 2, k0=k0, chunk_wait=(mid_ready, FT * f + k1))

            def batch(name, b, parts, wait=None):
                n = TR0[name] + b
                if n >= 2:
                    pe.wait_ge(tr_saved, n - 1)
                if wait:
                    pe.wait_ge(*wait)
                for src, c0 in parts:
                    r, w = src.shape[0], src.shape[1]
                    last = pe.transpose(bank[6 + n % 2][0:w, c0:c0 + r], src, ident[0:r, 0:r])
                last.then_inc(tr_ready, 1)

            def norm_sum(name):
                n = NORM[name]
                pe.wait_ge(sq_added, ADD0[name] + NORMS[n][1] - 1)
                if n:
                    pe.wait_ge(root_ready, n)
                pe.matmul(bank[5][:, :], neg_ones[:, :], sq_sum[:, :], start=True, stop=True)\
                    .then_inc(sum_ready, 1)

            def norm_sum2():
                pe.wait_ge(sq2_added, KT - 1)
                pe.matmul(bank[4][:, :], neg_ones[:, :], sq_sum2[:, :], start=True, stop=True)\
                    .then_inc(sum2_ready, 1)

            def softmax(name):
                for nxt, cur in pairs(session(name)):
                    for i in range(4):
                        if nxt:
                            j = 4 * nxt["head"] + i
                            if j >= 4:
                                pe.wait_ge(scores_read, j - 3)
                            dst = bank[2 + j % 4][:, 0:nxt["keys"][i]]
                            q = nxt["q"][:, P * i:P * (i + 1)]
                            last = pe.matmul(dst, q, nxt["k"][:, 0:nxt["keys"][i]], start=True,
                                             stop=True)
                            if nxt["mask"]:
                                last = pe.matmul(bank[2 + j % 4][:, P * i:P * (i + 1)], ident[:, :],
                                                 causal_neg[:, :], start=False, stop=True,
                                                 skip_group_check=True)
                            last.then_inc(scores_ready, 1)
                        if cur and i < cur["turns"]:
                            t = cur["turn"] + i
                            if t >= 2:
                                pe.wait_ge(pT_saved, t - 1)
                            first = i if cur["causal"] else 0
                            for qi in range(first, NT):
                                pe.wait_ge(probs_normed, 4 * cur["head"] + qi + 1)
                                last = pe.transpose(bank[6 + t % 2][:, P * qi:P * (qi + 1)],
                                                    probs[:, cur["head"] % 2, qi, P * i:P * (i + 1)],
                                                    ident[:, :])
                            last.then_inc(pT_ready, 1)
                        if cur and 1 <= i:
                            values(cur, i - 1)
                    if cur and cur["turns"] == 4:
                        values(cur, 3)

            def values(h, kj):
                if kj >= h["turns"]:
                    return
                pe.wait_ge(pT_saved, h["turn"] + kj + 1)
                if kj == 0 and h["head"] >= 2:
                    pe.wait_ge(out_saved, h["head"] - 1)
                    if h["head"] - 2 >= HEAD0["mem_a"]:
                        pe.wait_ge(out_low, h["head"] - 1 - HEAD0["mem_a"])
                q0 = query0(h, kj)
                last = pe.matmul(bank[h["head"] % 2][h["part"]:h["part"] + HD, q0:SEQ], h["v"](kj),
                                 probsT[:, h["head"] % 2, kj, q0:SEQ], start=kj == 0,
                                 stop=True, skip_group_check=True)
                if kj == h["turns"] - 1:
                    last.then_inc(out_ready, 1)

            def sb_qk(j):
                n, r, kj, q0 = sb_step(j)
                if j >= 5:
                    pe.wait_ge(sb_weights, j - 4)
                b = SB_BANK(j)
                k = head_rows(qkv[:, 16:20, :], n)[:, P * kj:P * (kj + 1)]
                pe.matmul(b[:, q0:SEQ], k, head_rows(qkv[:, 12:16, :], n)[:, q0:SEQ], start=True,
                          stop=True, skip_group_check=True)
                pe.matmul(b[:, q0:q0 + P], ident[:, :], strict_neg[:, :], start=False, stop=True,
                          skip_group_check=True).then_inc(sb_scores, 1)

            def sb_tail_sum(j):
                n, r, kj, q0 = sb_step(j)
                pe.wait_ge(sb_plus, j + 1)
                b = SB_BANK(j)
                last = pe.matmul(b[:, q0:SEQ], neg_upper[:, :], probs[:, n % 2, r, q0:SEQ],
                                 start=False, stop=True, skip_group_check=True)
                for older in range(r):
                    p0 = P * (3 - older)
                    last = pe.matmul(b[:, p0:SEQ], neg_ones[:, :], probs[:, n % 2, older, p0:SEQ],
                                     start=False, stop=True, skip_group_check=True)
                last.then_inc(sb_tail, 1)

            def sb_values(n):
                if n >= 2:
                    pe.wait_ge(sb_saved, n - 1)
                pe.wait_ge(sb_weights, 4 * n + 4)
                part = HD * (n % 2)
                for kj in range(4):
                    last = pe.matmul(bank[n % 2][part:part + HD, P * kj:SEQ],
                                     v_tok[:, kj, 512 + HD * n:512 + HD * (n + 1)],
                                     probsT[:, n % 2, kj, P * kj:SEQ], start=kj == 0, stop=True,
                                     skip_group_check=True)
                last.then_inc(sb_out, 1)

            def ada_sum(cols, which):
                for j in cols:
                    last = pe.matmul(bank[5][:, j:j + 1], ada_acc[:, P * j:P * (j + 1)], one_col,
                                     start=True, stop=True)
                last.then_inc(mod_summed, 1)

            pe.wait_ge(consts_set, 13)
            pe.wait_ge(vec_loaded, 16 * (len(VECTORS) + 1))
            sizes = [N_VEC, 48] + [2 * CT] * 6
            batch("vec", 0, [(vec_rows[0:sizes[i], i, :], P * i) for i in range(2)])
            pe.wait_ge(mem_normed, 2)
            for k in range(KT):
                batch("mem", k, [(mem_tok[:, t, P * k:P * (k + 1)], P * t) for t in range(2)])

            def turn_x(tiles):
                for k in tiles:
                    if k >= 4:
                        pe.wait_ge(x_saved, k - 3)
                    for t in range(NT):
                        last = pe.transpose(bank[4 + k % 4][:, P * t:P * (t + 1)],
                                            x_tok[:, t, P * k:P * (k + 1)], ident[:, :])
                    last.then_inc(x_turned, 1)

            def mem_chunk(c):
                l = c // 2
                chunk(c, c % 2, KT, CHUNK_COLS, lambda k: (mem_hi[:, l, k, :], mem_lo[:, l, k, :]),
                      g=c, gslot=c % 2, n=NMEM, chunk_wait=(mem_split, l + 1))

            pe.wait_ge(x_loaded, 16)
            pe.wait_ge(tr_saved, TR0["conv"])
            turn_x(range(4))
            mem_chunk(0)
            turn_x(range(4, KT))
            mem_chunk(1)
            pe.wait_ge(x_saved, KT)
            pe.wait_ge(conv_loaded, 16 * 4 * len(CONVS))
            for b in range(2):
                batch("conv", b, [(vec_rows[0:sizes[i], i, :], P * (i - 2 - 3 * b))
                                  for i in range(2 + 3 * b, 5 + 3 * b)])
            norm_sum("mix")
            mem_chunk(2)
            mem_chunk(3)
            for l, name in enumerate(("vm_a", "vm_b")):
                batch(name, 0, [(vmT[:, l, m, P * t:P * (t + 1)], NMEM * t + P * m)
                                for t in range(2) for m in range(2)], wait=(group_free, 2 * l + 2))
            pe.wait_ge(root_ready, 1)
            pe.wait_ge(ada_added, 8)
            ada_sum(range(16), 0)
            gemm_pairs("w_in", 6, act, normed("w_in"))
            pe.wait_ge(ada_added, 24)
            pe.wait_ge(mod_ready, 1)
            ada_sum(range(16, 48), 1)
            pe.wait_ge(group_free, G0["w_out"])
            for b in range(8):
                half, t = b // 4, b % 4
                batch("v_l0", b, [(qkv[:, 8 + 12 * half + m, P * t:P * (t + 1)], P * m) for m in range(4)],
                      wait=(mod_ready, 2) if b == 0 else None)
            pe.wait_ge(tr_saved, TR0["v_l0"] + 8)
            pe.wait_ge(q_scaled, 2)
            softmax("rel")
            pe.wait_ge(out_saved, 8)
            sb_qk(0)
            sb_qk(1)
            for j in range(SB_STEPS):
                if j + 2 < SB_STEPS:
                    sb_qk(j + 2)
                sb_tail_sum(j)
                if j % 4 == 1 and j > 4:
                    sb_values(j // 4 - 1)
                if j == 4:
                    norm_sum("oa")
            sb_values(7)
            norm_sum("ob")
            gemm_pairs("w_out", 2, o_0, normed("w_out"))
            norm_sum("ffn0")
            gemm_pairs("up0", FT // 2, act, normed("up0"))
            gemm_down(0)

            def both_sums():
                norm_sum("final_g")
                norm_sum2()

            for j, (_, n, _) in enumerate(A_IN):
                chunk(C0["a_in"] + j, j % 2, KT, n, act, g=G0["a_in"] + j, gslot=j % 2,
                      tile_wait=gained("a_in") if j == 0 else None,
                      between=both_sums if j == 0 else None)
                if j == 5:
                    batch("ws", 0, [(ws_raw[:, g, :], P * g) for g in range(GROUPS)],
                          wait=(gm_loaded, 32))
                    for b in range(8):
                        t, half = b // 2, b % 2
                        batch("v_a", b, [(z_a[:, 6 + 3 * half + m, P * t:P * (t + 1)], P * m)
                                         for m in range(3)], wait=(gelu_done, 3))
            pe.wait_ge(v_normed, 4)
            for ct in range(6):
                if ct >= 2:
                    pe.wait_ge(gm_biased, gm_count(ct - 2))
                for lo, hi, g in gm_parts(ct):
                    for t in range(NT):
                        last = pe.matmul(bank[4 + ct % 2][lo:hi, P * t:P * (t + 1)],
                                         vtok_a[:, t, P * ct + lo:P * ct + hi], wsT[:, g, :],
                                         start=True, stop=True, skip_group_check=True)
                last.then_inc(gm_ready, 1)
            pe.wait_ge(gm_biased, gm_count(5))
            pe.wait_ge(group_free, G0["a_out"])
            pe.wait_ge(zq_scaled, 2)
            pe.wait_ge(mem_back, 32)
            softmax("mem_a")
            pe.wait_ge(out_low, 4)
            gemm_pairs("a_out", 2, lambda k: (o_hi_a[:, k, :], o_lo_a[:, k, :]),
                       lambda k: (gm_split, k + 1) if k < 6 else (out_low, 2 * (k - 5)))
            gemm_pairs("up1", FT // 2, act, gained("up1"), between=lambda: norm_sum("a2"))
            gemm_down(1)
            gemm_pairs("b_q", 2, act, gained("b_q"), between=lambda: norm_sum("b1"))

            def kvm(k):
                return kvm_hi[:, k, :], kvm_lo[:, k, :]

            gemm_pairs("kv", 2, kvm, gained("kv"))
            for j, (_, n) in enumerate(KV_TAIL):
                chunk(C0["kv"] + 4 + j, j % 2, KT, n, kvm, g=G0["kv"] + 4 + j, gslot=j % 2)
            pe.wait_ge(group_free, G0["b_out"])
            for b in range(8):
                t, half = b // 2, b % 2
                batch("v_b", b, [(kv_b[:, 6 + 3 * half + m, P * t:P * (t + 1)], P * m) for m in range(3)])
            batch("f", 0, [(f_rows[:, 1, P * t:P * (t + 1)], FOX * t) for t in range(NT)], wait=(f_plus, 1))
            pe.wait_ge(tr_saved, TR0["f"] + 1)
            pe.wait_ge(tri_set, 2)
            for t in range(NT):
                last = pe.matmul(bank[4][0:FOX, P * t:SEQ], lfT[:, t, :], triext[:, 0:SEQ - P * t],
                                 start=t == 0, stop=True, skip_group_check=True)
            last.then_inc(f_summed, 1)
            pe.wait_ge(f_saved, 1)
            softmax("fox")
            pe.wait_ge(mem_back, 64)
            softmax("mem_b")
            pe.wait_ge(out_low, 20)
            gemm_pairs("b_out", 2, lambda k: (o_hi_b[:, k, :], o_lo_b[:, k, :]),
                       lambda k: (out_low, 4 + 2 * (k + 1)))
            gemm_pairs("up2", FT // 2, act, gained("up2"), between=lambda: norm_sum("b2"))
            gemm_down(2)
            norm_sum("final")
            for b in range(8):
                t, half = b // 2, b % 2
                batch("out", b, [(y[:, 4 * half + m, P * t:P * (t + 1)], P * m) for m in range(4)],
                      wait=(y_ready, 4 * half + 4))

        @block.scalar
        def _(act):
            def split_w(c, slot, count, n=2048):
                act.wait_ge(w_loaded[slot], count)
                if not isinstance(c, int) or c >= 2:
                    act.wait_ge(chunk_done, c - 1)
                act.activation(w_hi[slot][:, 0:n], w_stage[slot][:, 0:n], ACT.Copy).then_inc(w_hi_done, 1)

            def split_at(c, n=2048):
                split_w(c, c % 2, 16 * (c // 2 + 1), n)

            def split_loop(c0, i, s):
                split_w(c0 + 2 * i + s, s, 16 * i + 16 * (c0 // 2 + 1))

            def squares(name, tile, ready):
                n, count = NORM[name], NORMS[NORM[name]][1]
                for t in range(count):
                    square(name, t, tile(t), ready(t))

            def square(name, t, src, ready):
                n = NORM[name]
                act.wait_ge(*ready)
                if t == 0:
                    if n:
                        act.wait_ge(sum_ready, n)
                    act.activation(sq_sum[:, :], src, ACT.Square).then_inc(sq_ready, 1)
                else:
                    if t >= 3:
                        act.wait_ge(sq_added, ADD0[name] + t - 2)
                    act.activation(squares_of(name, t), src, ACT.Square).then_inc(sq_ready, 1)

            def root(name):
                n, count = NORM[name], NORMS[NORM[name]][1]
                act.wait_ge(sum_ready, n + 1)
                act.activation(rms[:, :], bank[5][:, :], ACT.Sqrt, scale=-1.0 / (P * count), bias=eps)\
                    .then_inc(root_ready, 1)

            def high(name, t, dst, bias=None, buf=tmp):
                act.wait_ge(scaled, SPLIT0[name] + t + 1)
                act.activation(dst, buf[:, t % 4, :], ACT.Identity,
                               bias=bias if bias is not None else 0.0).then_inc(act_hi_done, 1)

            def gain_high(ph, t, dst, col):
                act.activation(dst[:, t, :], x[:, t, :], ACT.Copy, scale=col).then_inc(gain_hi, 1)

            def exps(h, i):
                j = 4 * h["head"] + i
                act.wait_ge(scores_read, j + 1)
                if h["head"] >= 2 and i == 0:
                    act.wait_ge(pT_ready, TURN0[h["head"] - 1])
                n = h["keys"][i]
                act.activation(probs[:, h["head"] % 2, i, 0:n], tmp[:, j % 4, 0:n], ACT.Exp, scale=-1.0,
                               bias=neg_max[:, j % 8:j % 8 + 1],
                               accum_out=row_sum[:, j % 8:j % 8 + 1]).then_inc(probs_ready, 1)

            def save_pT(h, kj):
                t = h["turn"] + kj
                act.wait_ge(pT_ready, t + 1)
                if h["head"] >= 2 and kj == 0:
                    act.wait_ge(out_ready, h["head"] - 1)
                q0 = query0(h, kj)
                act.activation(probsT[:, h["head"] % 2, kj, q0:SEQ], bank[6 + t % 2][:, q0:SEQ],
                               ACT.Copy).then_inc(pT_saved, 1)

            def softmax(name):
                for nxt, cur in pairs(session(name)):
                    for i in range(4):
                        if nxt:
                            exps(nxt, i)
                        if cur and i < cur["turns"]:
                            save_pT(cur, i)
                    if cur:
                        act.wait_ge(out_ready, cur["head"] + 1)
                        act.activation(cur["out"], bank[cur["head"] % 2][cur["part"]:cur["part"] + HD, :],
                                       ACT.Copy).then_inc(out_saved, 1)

            def softplus(t, clamped, exped, logged, n):
                act.wait_ge(clamped, n)
                act.activation(t, t, ACT.Exp).then_inc(exped, 1)
                act.wait_ge(exped, n)
                act.activation(t, t, ACT.Ln, bias=1.0).then_inc(logged, 1)

            def up(f):
                c0, g0, n0 = C0[f"up{f}"], G0[f"up{f}"], FT // 2 * f
                vb = P * (3 + 2 * f)
                act.preload_act_table(ACT.Silu)
                with act.Fori(0, FT // 2) as i:
                    for s in range(2):
                        split_loop(c0 + 2, i, s)
                        for m in range(2):
                            if f and m:
                                act.wait_ge(group_free, 2 * i + s + g0 + 1)
                            elif f:
                                act.wait_ge(up_scaled, 2 * i + s + 2 * n0 - FT + 1)
                            elif m == 0:
                                act.wait_ge(tile0_done, 2 * i + s + first_tiles(g0))
                            else:
                                act.wait_ge(chunk_done, 2 * i + s + c0 + 1)
                            if s == 0 and m == 0:
                                act.wait_ge(w_ready, 2 * i + c0 + 3)
                            w2 = vec[:, bass.ds(2 * i + vb + FT * s + m, 1)]
                            b = vec[:, bass.ds(2 * i + vb + CT + FT * s + m, 1)]
                            act.activation(conv_tile(f, i, s, m), conv_src(f, s, m)[:, :],
                                           ACT.Identity, scale=w2, bias=b).then_inc(tap_started, 1)
                    for m in range(2):
                        act.wait_ge(*taps(f, i, 0, m))
                        act.activation(tmp[:, m, :], tmp[:, m, :], ACT.Silu).then_inc(gate_done, 1)
                    for m in range(2):
                        act.wait_ge(mid_done, 2 * n0 + 2 * i + m + 1)
                        act.activation(mid_hi[:, bass.ds(2 * i + m, 1), :], tmp[:, m, :], ACT.Copy)\
                            .then_inc(mid_hi_done, 1)

            def next_tile(name, ph, t, move):
                src = x[:, t, :]
                if not move:
                    square(name, t, src, updated(ph, t))
                    return
                act.wait_ge(*updated(ph, t))
                gain_high(move[0], t, move[1], move[2](t))
                square(name, t, src, updated(ph, t))
                if name == "final_g":
                    g = gain("final_g", t)
                    dst = sq_sum2[:, :]
                    if t:
                        if t >= 3:
                            act.wait_ge(sq2_added, t - 2)
                        dst = tmp[:, t % 2, :]
                    act.activation(dst, src, ACT.Square, scale=g).then_inc(sq2_ready, 1)

            def updated(ph, t):
                if t % 2:
                    return group_free, G0[ph] + t // 2 + 1
                return x_ready, X0[ph] + t // 2 + 1

            def down(f, name, move=None):
                def split_next(n):
                    if C0[f"down{f}"] + n < N_CHUNKS:
                        split_at(C0[f"down{f}"] + n,
                                 6 * CHUNK_COLS if n % 3 == 2 and n < 12 else 2048)
                for g in range(4):
                    for r in range(2):
                        split_next(3 * g + r + 2)
                    for m in range(2):
                        t = 2 * g + m
                        next_tile(name, f"down{f}", t, move)
                    split_next(3 * g + 4)

            def out_phase(ph, name, move=None):
                for g in range(4):
                    for m in range(2):
                        t = 2 * g + m
                        next_tile(name, ph, t, move)
                    split_at(C0[ph] + g + 2)

            load_vectors(act, VECTORS[1::2])
            act.dma_start(vec_rows[0:48, 1, :], a["b_ada"].rearrange("o (k p) -> (o k) p", p=P))\
                .then_inc(vec_loaded, 16)
            act.wait_ge(mem_loaded, 16)
            act.wait_ge(consts_set, 13)
            for t in range(2):
                if t:
                    act.wait_ge(mem_ss, t)
                act.activation(sq_junk[:, :], mem_tok[:, t, :], ACT.Square,
                               accum_out=tok_ss[:, t:t + 1]).then_inc(mem_ss, 1)
            act.wait_ge(mem_ss, 2)
            act.activation(tok_rms[:, 0:2], tok_ss[:, 0:2], ACT.Sqrt, scale=1.0 / D, bias=eps)\
                .then_inc(mem_root, 1)
            act.wait_ge(tr_saved, TR0["vec"] + 1)
            act.activation(sig_c, vec[:, VEC0["c"]:VEC0["c"] + 8], ACT.Silu).then_inc(c_act, 1)
            for k in range(KT):
                act.wait_ge(tr_ready, TR0["mem"] + k + 1)
                for l, name in enumerate(("a_mem_norm_2", "b_mem_norm_2")):
                    last = act.activation(mem_scaled[:, l, k, :], bank[6 + (TR0["mem"] + k) % 2][:, 0:NMEM],
                                          ACT.Copy, scale=gain(name, k))
                last.then_inc(tr_saved, 1)
            split_at(0)
            split_at(1)
            act.wait_ge(tr_saved, TR0["mem"] + 8)

            def high_mem(l):
                act.activation(mem_hi[:, l, :, :], mem_scaled[:, l, :, :], ACT.Copy).then_inc(mem_hi_done, 1)

            def save_x(tiles):
                for k in tiles:
                    act.wait_ge(x_turned, k + 1)
                    act.activation(x[:, k, :], bank[4 + k % 4][:, :], ACT.Copy).then_inc(x_saved, 1)
                    square("mix", k, x[:, k, :], (x_saved, k + 1))

            high_mem(0)
            save_x(range(4))
            high_mem(1)
            split_at(2)
            save_x(range(4, KT))
            for c in range(3, 5):
                split_at(c)
            root("mix")
            split_at(5)
            for t in range(KT):
                high("w_in", t, act_hi[:, t, :], bias=modv(SHIFT_MIX, t))
            with act.Fori(0, 6) as i:
                for s in range(2):
                    split_loop(C0["w_in"] + 2, i, s)
            for n, t in enumerate((0, 12)):
                act.wait_ge(group_free, G0["w_in"] + t // 2 + 2)
                act.activation(qkv[:, t:t + 4, :], qkv[:, t:t + 4, :], ACT.Copy, scale=HD ** -0.5)\
                    .then_inc(q_scaled, 1)
            act.wait_ge(chunk_done, C0["w_out"])
            softmax("rel")
            squares("oa", lambda t: qkv[:, 8 + t, :], lambda t: (out_saved, 2 * (t + 1)))
            act.preload_act_table_set("natural_log_exp_and_others")
            for j in range(SB_STEPS + 2):
                if j < SB_STEPS:
                    n, r, kj, q0 = sb_step(j)
                    softplus(tmp[:, j % 4, q0:SEQ], sb_clamped, sb_exped, sb_logged, j + 1)
                if j >= 2:
                    i = j - 2
                    n, r, kj, q0 = sb_step(i)
                    act.wait_ge(sb_tail, i + 1)
                    if n >= 2 and r == 0:
                        act.wait_ge(sb_out, n - 1)
                    act.activation(probsT[:, n % 2, kj, q0:SEQ], SB_BANK(i)[:, q0:SEQ], ACT.Exp)\
                        .then_inc(sb_weights, 1)
                if j % 4 == 3 and j >= 7:
                    sb_save(act, j // 4 - 1)
                if j == 6:
                    root("oa")
                    for t in range(4):
                        high("w_out", t, o_hi_0[0][:, t, :], buf=rel[0])
                    act.preload_act_table_set("natural_log_exp_and_others")
            sb_save(act, 7)
            squares("ob", lambda t: qkv[:, 20 + t, :], lambda t: (sb_saved, 2 * (t + 1)))
            root("ob")
            for t in range(4):
                high("w_out", 4 + t, o_hi_0[1][:, t, :])
            out_phase("w_out", "ffn0")
            root("ffn0")
            act.wait_ge(chunk_done, C0["up0"])
            for t in range(KT):
                high("up0", t, act_hi[:, t, :], bias=modv(SHIFT_FFN, t))
            up(0)
            down(0, "final_g", ("a_in", act_hi, lambda t: gain_a1[:, t:t + 1]))
            root("final_g")
            act.wait_ge(mean2_ready, 1)
            act.activation(rms2[:, :], rms2[:, :], ACT.Sqrt, scale=-1.0 / D, bias=eps)\
                .then_inc(root2_ready, 1)
            for j, (_, n, tiles) in enumerate(A_IN):
                c = C0["a_in"] + j + 2
                split_at(c, KT * A_IN[j + 2][1] if j < 6 else 2048)
                act.wait_ge(group_free, G0["a_in"] + j + 1)
                zt = z_a[:, tiles[0]:tiles[-1] + 1, :]
                if n == P:
                    act.activation(zt, zt, ACT.Copy, scale=HD ** -0.5).then_inc(zq_scaled, 1)
                else:
                    act.activation(zt, zt, ACT.Gelu_apprx_tanh).then_inc(gelu_done, 1)
                if j == 5:
                    for t in range(NT):
                        act.wait_ge(tr_saved, TR0["v_a"] + 2 * t + 2)
                        if t:
                            act.wait_ge(v_ss, t)
                        act.activation(vsq_junk[:, :], vtok_a[:, t, :], ACT.Square,
                                       accum_out=tok_ss[:, t:t + 1]).then_inc(v_ss, 1)
                    act.wait_ge(v_ss, 4)
                    act.activation(tok_rms, tok_ss, ACT.Sqrt, scale=1.0 / TOK, bias=eps)\
                        .then_inc(v_root, 1)
            act.preload_act_table(ACT.Exp)
            for t in range(6):
                act.wait_ge(gm_done, t + 1)
                act.activation(o_hi_a[:, t, :], z_a[:, t, :], ACT.Copy).then_inc(gm_hi, 1)
            softmax("mem_a")
            out_phase("a_out", "a2", ("up1", act_hi, lambda t: gain("a_norm2_2", t)))
            root("a2")
            up(1)
            down(1, "b1", ("b_q", act_hi, lambda t: gain("b_norm1_2", t)))
            root("b1")
            act.wait_ge(chunk_done, C0["b_q"])
            for t in range(KT):
                gain_high("kv", t, kvm_hi, gain("kv_norm_2", t))
            with act.Fori(0, 2) as i:
                for s in range(2):
                    split_loop(C0["b_q"] + 2, i, s)
            with act.Fori(0, 2) as i:
                for s in range(2):
                    split_loop(C0["kv"] + 2, i, s)
            for j in range(4):
                c = C0["kv"] + 6 + j
                split_at(c, KT * KV_TAIL[2 + j][1] if j < 2 else 2048)
            act.preload_act_table_set("natural_log_exp_and_others")
            softplus(f_rows[:, 2, :], f_clamped, f_exped, f_logged, 1)
            softmax("fox")
            softmax("mem_b")
            out_phase("b_out", "b2", ("up2", act_hi, lambda t: gain("b_norm2_2", t)))
            root("b2")
            up(2)
            down(2, "final")
            root("final")

        @block.vector
        def _(dve):
            def split_w(c, slot, n=2048):
                dve.wait_ge(w_hi_done, c + 1)
                dve.tensor_tensor(w_lo[slot][:, 0:n], w_stage[slot][:, 0:n],
                                  w_hi[slot][:, 0:n].bitcast(FP32), ALU.subtract).then_inc(w_ready, 1)

            def copy_group(c, tile0, slot, dst, n=SEQ):
                dve.wait_ge(tile0_done, tile0)
                dve.tensor_copy(dst(0), bank[2 * slot][:, 0:n])
                dve.wait_ge(chunk_done, c + 1)
                dve.tensor_copy(dst(1), bank[2 * slot + 1][:, 0:n]).then_inc(group_free, 1)

            def norm_group(c, tile0, slot, dst, norm, scale=1.0):
                dve.wait_ge(tile0_done, tile0)
                norm_tile(dst(0), bank[2 * slot], norm, scale)
                dve.wait_ge(chunk_done, c + 1)
                norm_tile(dst(1), bank[2 * slot + 1], norm, scale).then_inc(group_free, 1)

            def norm_tile(dst, src, norm, scale=1.0):
                return dve.scalar_tensor_tensor(out=dst, in0=src[:, :], scalar=scale, in1=norm[:, :],
                                                op0=ALU.mult, op1=ALU.mult)

            def add_squares(name, t):
                dve.wait_ge(sq_ready, SQ0[name] + t + 1)
                if t > 1:
                    dve.wait_ge(sq_added, ADD0[name] + t - 1)
                dve.tensor_tensor(sq_sum[:, :], sq_sum[:, :], squares_of(name, t), ALU.add)\
                    .then_inc(sq_added, 1)

            def invert(name):
                n = NORM[name]
                dve.wait_ge(root_ready, n + 1)
                dve.reciprocal(rms[:, :], rms[:, :]).then_inc(rms_ready, 1)
                dve.wait_ge(rms_ready, n + 1)

            def scale_tiles(ph, tiles, src, col, dst, bias=None, buf=tmp):
                def low(t):
                    dve.wait_ge(act_hi_done, SPLIT0[ph] + t + 1)
                    hi = dst[0][:, t - tiles[0], :].bitcast(FP32)
                    lo = dst[1][:, t - tiles[0], :]
                    if bias is None:
                        dve.tensor_tensor(lo, buf[:, t % 4, :], hi, ALU.subtract)\
                            .then_inc(act_ready, 1)
                    else:
                        dve.scalar_tensor_tensor(out=lo, in0=buf[:, t % 4, :],
                                                 scalar=bias(t), in1=hi, op0=ALU.add,
                                                 op1=ALU.subtract).then_inc(act_ready, 1)
                for n, t in enumerate(tiles):
                    dve.scalar_tensor_tensor(out=buf[:, t % 4, :], in0=src(t), scalar=col(t),
                                             in1=rms[:, :], op0=ALU.mult, op1=ALU.mult)\
                        .then_inc(scaled, 1)
                    if n:
                        low(t - 1)
                low(tiles[-1])

            def gain_low(ph, t, dst, col):
                dve.wait_ge(gain_hi, GAIN0[ph] + t + 1)
                dve.scalar_tensor_tensor(out=dst[1][:, t, :], in0=x[:, t, :], scalar=col,
                                         in1=dst[0][:, t, :].bitcast(FP32), op0=ALU.mult,
                                         op1=ALU.subtract).then_inc(gain_ready, 1)

            def tr_bank(name, b):
                n = TR0[name] + b
                dve.wait_ge(tr_ready, n + 1)
                return bank[6 + n % 2]

            def shift_scores(h, i):
                j = 4 * h["head"] + i
                n = h["keys"][i]
                dve.wait_ge(scores_ready, j + 1)
                if j >= 4:
                    dve.wait_ge(probs_ready, j - 3)
                dve.tensor_tensor_reduce(out=tmp[:, j % 4, 0:n], in0=bank[2 + j % 4][:, 0:n],
                                         in1=h["bias"](i), scale=-1.0, scalar=3.0e38, op0=ALU.add,
                                         op1=ALU.min, accum_out=neg_max[:, j % 8:j % 8 + 1])\
                    .then_inc(scores_read, 1)

            def normalize(h, i):
                j = 4 * h["head"] + i
                n = h["keys"][i]
                dve.wait_ge(probs_ready, j + 1)
                inv = row_inv[:, j % 8:j % 8 + 1]
                dve.reciprocal(inv, row_sum[:, j % 8:j % 8 + 1]).then_inc(inv_ready, 1)
                dve.wait_ge(inv_ready, j + 1)
                p = probs[:, h["head"] % 2, i, 0:n]
                dve.tensor_scalar(p, p, inv, None, ALU.mult).then_inc(probs_normed, 1)

            def save_low(h):
                if h["low"] is None:
                    return
                dve.wait_ge(out_saved, h["head"] + 1)
                dve.tensor_tensor(h["low"], bank[h["head"] % 2][h["part"]:h["part"] + HD, :],
                                  h["out"].bitcast(FP32), ALU.subtract).then_inc(out_low, 1)

            def softmax(name, before=None):
                for h, done in pairs(session(name)):
                    if before and h and h["head"] % 4 == 0:
                        before(h["head"] // 4)
                    for i in range(4):
                        if h:
                            shift_scores(h, i)
                            if i:
                                normalize(h, i - 1)
                    if h:
                        normalize(h, 3)
                    if done:
                        save_low(done)

            def ada(n, part, k, load_count, first=False):
                dve.wait_ge(ada_loaded[n], load_count)
                acc = ada_acc[:, part * 2048:(part + 1) * 2048]
                if first:
                    dve.tensor_scalar(acc, ada_stage[n][:, :], k, None, ALU.mult).then_inc(ada_added, 1)
                    return
                dve.scalar_tensor_tensor(out=acc, in0=ada_stage[n][:, :], scalar=k, in1=acc,
                                         op0=ALU.mult, op1=ALU.add).then_inc(ada_added, 1)

            def mod_columns(lo, hi, n, scale):
                dve.wait_ge(mod_summed, n)
                dve.tensor_tensor(mod[:, lo:hi], bank[5][:, lo:hi], vec[:, P + lo:P + hi], ALU.add)\
                    .then_inc(mod_added, 1)
                dve.wait_ge(mod_added, n)
                dve.tensor_scalar(mod[:, 8 * scale:8 * scale + 8], mod[:, 8 * scale:8 * scale + 8],
                                  1.0, None, ALU.add).then_inc(mod_ready, 1)
                dve.wait_ge(mod_ready, n)

            def up(f):
                c0, g0, n0 = C0[f"up{f}"], G0[f"up{f}"], FT // 2 * f
                va = P * (2 + 2 * f)
                with dve.Fori(0, FT // 2) as i:
                    for s in range(2):
                        split_w(2 * i + s + c0 + 2, s)
                        if f:
                            for m in range(2):
                                if m == 0:
                                    dve.wait_ge(tile0_done, 2 * i + s + first_tiles(g0))
                                else:
                                    dve.wait_ge(chunk_done, 2 * i + s + c0 + 1)
                                if m == 0 and s:
                                    dve.wait_ge(*taps(f, i, 0, 1))
                                norm_tile(conv_src(f, s, m), bank[2 * s + m], rms)\
                                    .then_inc(group_free if m else up_scaled, 1)
                            dve.wait_ge(group_free, 2 * i + s + g0 + 1)
                        for m in range(2):
                            n = 2 * s + m
                            t, b = conv_tile(f, i, s, m), conv_src(f, s, m)
                            if len(t.shape) == 3:
                                t = t.rearrange("p o n -> p (o n)")
                            w0 = vec[:, bass.ds(2 * i + va + FT * s + m, 1)]
                            w1 = vec[:, bass.ds(2 * i + va + CT + FT * s + m, 1)]
                            dve.wait_ge(tap_started, 4 * i + 4 * n0 + n + 1)
                            dve.scalar_tensor_tensor(out=t[:, 1:SEQ], in0=b[:, 0:SEQ - 1], scalar=w1,
                                                     in1=t[:, 1:SEQ], op0=ALU.mult, op1=ALU.add)\
                                .then_inc(tap_added, 1)
                            dve.wait_ge(tap_added, 4 * i + 4 * n0 + n + 1)
                            dve.scalar_tensor_tensor(out=t[:, 2:SEQ], in0=b[:, 0:SEQ - 2], scalar=w0,
                                                     in1=t[:, 2:SEQ], op0=ALU.mult, op1=ALU.add)\
                                .then_inc(group_free if m and not f else taps_done, 1)
                    for m in range(2):
                        dve.wait_ge(gate_done, 2 * i + 2 * n0 + m + 1)
                        dve.wait_ge(*taps(f, i, 1, m))
                        dve.tensor_tensor(tmp[:, m, :], tmp[:, m, :], conv_tile(f, i, 1, m), ALU.mult)\
                            .then_inc(mid_done, 1)
                    for m in range(2):
                        dve.wait_ge(mid_hi_done, 2 * i + 2 * n0 + m + 1)
                        dve.tensor_tensor(mid_lo[:, bass.ds(2 * i + m, 1), :], tmp[:, m, :],
                                          mid_hi[:, bass.ds(2 * i + m, 1), :].bitcast(FP32),
                                          ALU.subtract).then_inc(mid_ready, 1)

            def update(ph, g, c, gate):
                for m in range(2):
                    t = 2 * g + m
                    if m == 0:
                        dve.wait_ge(tile0_done, first_tiles(G0[ph] + g))
                    else:
                        dve.wait_ge(chunk_done, c + 1)
                    b = bank[2 * (g % 2) + m][:, :]
                    if gate is None:
                        last = dve.tensor_tensor(x[:, t, :], b, x[:, t, :], ALU.add)
                    else:
                        last = dve.scalar_tensor_tensor(out=x[:, t, :], in0=b, scalar=modv(gate, t),
                                                        in1=x[:, t, :], op0=ALU.mult, op1=ALU.add)
                    last.then_inc(group_free if m else x_ready, 1)

            def after(name, t, move):
                if move:
                    gain_low(move[0], t, move[1], move[2](t))
                if t:
                    add_squares(name, t)
                if t and name == "final_g":
                    dve.wait_ge(sq2_ready, t + 1)
                    if t > 1:
                        dve.wait_ge(sq2_added, t - 1)
                    dve.tensor_tensor(sq_sum2[:, :], sq_sum2[:, :], tmp[:, t % 2, :], ALU.add)\
                        .then_inc(sq2_added, 1)

            def out_phase(ph, name, gate=None, move=None):
                for g in range(4):
                    update(ph, g, C0[ph] + g, gate)
                    for t in range(max(0, 2 * g - 2), 2 * g):
                        after(name, t, move)
                    if g < 3:
                        split_w(C0[ph] + g + 2, g % 2)
                after(name, 6, move)
                after(name, 7, move)
                split_w(C0[ph] + 5, 1)
                invert(name)

            def down(f, name, gate=None, move=None):
                def split_next(n):
                    if C0[f"down{f}"] + n < N_CHUNKS:
                        split_w(C0[f"down{f}"] + n, n % 2,
                                6 * CHUNK_COLS if n % 3 == 2 and n < 12 else 2048)
                for g in range(4):
                    for r in range(2):
                        split_next(3 * g + r + 2)
                    update(f"down{f}", g, C0[f"down{f}"] + 3 * g + 2, gate)
                    for t in range(max(0, 2 * g - 2), 2 * g):
                        after(name, t, move)
                    if g < 3:
                        split_next(3 * g + 4)
                after(name, 6, move)
                after(name, 7, move)
                split_next(13)
                invert(name)

            def spatial_operands():
                dve.tensor_tensor(wsT[:, :, :], tr_bank("ws", 0)[:, :].rearrange("p (g t) -> p g t", t=P),
                                  tri[:, :].rearrange("p (o t) -> p o t", o=1).to_broadcast([P, GROUPS, P]),
                                  ALU.mult).then_inc(tr_saved, 1)
                dve.memset(zero_a[:, :], 0.0).then_inc(zero_set, 1)
                for b in range(8):
                    t, half = b // 2, b % 2
                    dve.tensor_copy(vtok_a[:, t, 384 * half:384 * (half + 1)], tr_bank("v_a", b)[:, 0:384])\
                        .then_inc(tr_saved, 1)
                dve.wait_ge(v_root, 1)
                dve.reciprocal(tok_rms, tok_rms).then_inc(v_rms, 1)
                dve.wait_ge(v_rms, 1)
                for t in range(NT):
                    dve.tensor_scalar(vtok_a[:, t, :], vtok_a[:, t, :], tok_rms[:, t:t + 1], None,
                                      ALU.mult).then_inc(v_normed, 1)

            def gm_low(ct):
                dve.wait_ge(gm_hi, ct + 1)
                dve.tensor_tensor(o_lo_a[:, ct, :], z_a[:, ct, :], o_hi_a[:, ct, :].bitcast(FP32),
                                  ALU.subtract).then_inc(gm_split, 1)

            dve.wait_ge(mem_root, 1)
            dve.reciprocal(tok_rms[:, 0:2], tok_rms[:, 0:2]).then_inc(mem_rms, 1)
            dve.wait_ge(mem_rms, 1)
            for t in range(2):
                dve.tensor_scalar(mem_tok[:, t, :], mem_tok[:, t, :], tok_rms[:, t:t + 1], None,
                                  ALU.mult).then_inc(mem_normed, 1)
            sizes = [N_VEC, 48] + [2 * CT] * 6
            src = tr_bank("vec", 0)
            for i in range(2):
                last = dve.tensor_copy(vec[:, P * i:P * i + sizes[i]], src[:, P * i:P * i + sizes[i]])
            last.then_inc(tr_saved, 1)
            dve.wait_ge(tr_saved, TR0["vec"] + 1)
            dve.tensor_tensor(gain_a1, vec[:, VEC0["final_g"]:VEC0["final_g"] + 8],
                              vec[:, VEC0["a_norm1_2"]:VEC0["a_norm1_2"] + 8], ALU.mult)\
                .then_inc(gain_a1_set, 1)

            def ada_scales(k):
                if k:
                    dve.wait_ge(ada_added, k)
                ada(k % 2, 0, sig_c[:, k:k + 1], 16 * (k // 2 + 1), first=k == 0)

            dve.wait_ge(c_act, 1)
            ada_scales(0)
            ada_scales(1)
            split_w(0, 0)
            split_w(1, 1)

            def low_mem(l):
                dve.wait_ge(mem_hi_done, l + 1)
                dve.tensor_tensor(mem_lo[:, l, :, :], mem_scaled[:, l, :, :],
                                  mem_hi[:, l, :, :].bitcast(FP32), ALU.subtract).then_inc(mem_split, 1)

            mem_dst = [kmT_0[:, 0, :, :], vmT[:, 0, :, :], kmT_0[:, 1, :, :], vmT[:, 1, :, :]]

            def mem_group(c):
                split_w(c + 2, c % 2)
                copy_group(c, first_tiles(c), c % 2, lambda m: mem_dst[c][:, m, :], n=NMEM)

            low_mem(0)
            ada_scales(2)
            for t in range(1, 4):
                add_squares("mix", t)
            low_mem(1)
            ada_scales(3)
            mem_group(0)
            ada_scales(4)
            for t in range(4, KT):
                add_squares("mix", t)
            mem_group(1)
            for b in range(2):
                src = tr_bank("conv", b)
                for i in range(2 + 3 * b, 5 + 3 * b):
                    c = P * (i - 2 - 3 * b)
                    last = dve.tensor_copy(vec[:, P * i:P * i + sizes[i]], src[:, c:c + sizes[i]])
                last.then_inc(tr_saved, 1)
            ada_scales(5)
            dve.wait_ge(rb_loaded, 16)
            dve.tensor_copy(rel_rows[:, 0:384], rb_rows[:, RB - 1:RB].to_broadcast([8, 384]))\
                .then_inc(rel_flat, 1)
            dve.tensor_copy(rel_rows[:, 384:RROW - 1], rb_rows[:, RB - 2:0:-1]).then_inc(rel_flat, 1)
            dve.memset(rel_rows[:, RROW - 1:RROW], 0.0).then_inc(rel_flat, 1)
            mem_group(2)
            ada_scales(6)
            mem_group(3)
            for l, name in enumerate(("vm_a", "vm_b")):
                dve.tensor_copy(vm_0[:, l, :, :].rearrange("p a b -> p (a b)"), tr_bank(name, 0)[:, :])\
                    .then_inc(tr_saved, 1)
            ada_scales(7)
            invert("mix")
            mod_columns(0, 16, 1, SCALE_MIX)
            scale_tiles("w_in", range(KT), lambda t: x[:, t, :], lambda t: modv(SCALE_MIX, t),
                        (act_hi, act_lo),
                        bias=lambda t: modv(SHIFT_MIX, t))
            for k in (0, 1):
                for s in range(2):
                    dve.wait_ge(ada_added, 2 * k + s + 7)
                    ada(s, 1 + s, sig_c[:, k:k + 1], 16 * (k + 5), first=k == 0)
            dve.wait_ge(mem_stored, 32)
            with dve.Fori(0, 6) as i:
                for s in range(2):
                    split_w(2 * i + s + C0["w_in"] + 2, s)
                    copy_group(2 * i + s + C0["w_in"], 2 * i + s + first_tiles(G0["w_in"]), s,
                               lambda m: qkv[:, bass.ds(4 * i + 2 * s + m, 1), :])
                    dve.wait_ge(ada_added, 2 * i + s + 11)
                    ada(s, 1 + s, stats[:, bass.ds(i + 38, 1)], 16 * i + 112)
            mod_columns(16, 48, 2, SCALE_FFN)
            for b in range(8):
                half, t = b // 4, b % 4
                dve.tensor_copy(v_tok[:, t, 512 * half:512 * half + 512], tr_bank("v_l0", b)[:, :])\
                    .then_inc(tr_saved, 1)
            def mask_rel(j):
                dve.wait_ge(rel_back, 16 * (j + 1))
                dve.memset(rel[j][0:HD, :, SEQ - HD:SEQ], NEG).then_inc(rel_masked, 1)
                dve.wait_ge(rel_masked, j + 1)

            softmax("rel", before=mask_rel)
            for t in range(1, 4):
                add_squares("oa", t)
            for j in range(SB_STEPS + 1):
                if j < SB_STEPS:
                    n, r, kj, q0 = sb_step(j)
                    dve.wait_ge(sb_scores, j + 1)
                    dve.tensor_scalar(tmp[:, j % 4, q0:SEQ], SB_BANK(j)[:, q0:SEQ], CLAMP, None,
                                      ALU.min).then_inc(sb_clamped, 1)
                if j >= 1:
                    i = j - 1
                    n, r, kj, q0 = sb_step(i)
                    dve.wait_ge(sb_logged, i + 1)
                    if n >= 2 and r == 0:
                        dve.wait_ge(sb_tail, 4 * (n - 1))
                    dve.tensor_tensor(probs[:, n % 2, r, q0:SEQ], SB_BANK(i)[:, q0:SEQ],
                                      tmp[:, i % 4, q0:SEQ], ALU.max).then_inc(sb_plus, 1)
                if j == 6:
                    invert("oa")
                    scale_tiles("w_out", range(4), lambda t: qkv[:, 8 + t, :],
                                lambda t: gain("g_a", t), (o_hi_0[0], o_lo_0[0]), buf=rel[0])
            for t in range(1, 4):
                add_squares("ob", t)
            invert("ob")
            scale_tiles("w_out", range(4, 8), lambda t: qkv[:, 16 + t, :],
                        lambda t: gain("g_b", t - 4), (o_hi_0[1], o_lo_0[1]))
            out_phase("w_out", "ffn0", GATE_MIX)
            scale_tiles("up0", range(KT), lambda t: x[:, t, :], lambda t: modv(SCALE_FFN, t),
                        (act_hi, act_lo),
                        bias=lambda t: modv(SHIFT_FFN, t))
            up(0)
            act_parts = (act_hi, act_lo)
            down(0, "final_g", GATE_FFN, ("a_in", act_parts, lambda t: gain_a1[:, t:t + 1]))
            dve.tensor_tensor(rms2[:, :], rms[:, :], rms[:, :], ALU.mult).then_inc(rms_squared, 1)
            dve.wait_ge(rms_squared, 1)
            dve.wait_ge(sum2_ready, 1)
            dve.tensor_tensor(rms2[:, :], bank[4][:, :], rms2[:, :], ALU.mult).then_inc(mean2_ready, 1)
            dve.wait_ge(root2_ready, 1)
            dve.reciprocal(rms2[:, :], rms2[:, :]).then_inc(rms2_ready, 1)
            dve.wait_ge(rms2_ready, 1)
            dve.tensor_tensor(rms2[:, :], rms2[:, :], rms[:, :], ALU.mult).then_inc(rms12_ready, 1)
            dve.wait_ge(rms12_ready, 1)
            for j, (_, n, tiles) in enumerate(A_IN):
                c = C0["a_in"] + j
                split_w(c + 2, j % 2, KT * A_IN[j + 2][1] if j < 6 else 2048)
                if n == P:
                    dve.wait_ge(chunk_done, c + 1)
                    norm_tile(z_a[:, tiles[0], :], bank[2 * (j % 2)], rms2).then_inc(group_free, 1)
                else:
                    norm_group(c, first_tiles(G0["a_in"] + j), j % 2,
                               lambda m: z_a[:, tiles[m], :], rms2)
                if j == 0:
                    for t in range(KT):
                        dve.scalar_tensor_tensor(out=x[:, t, :], in0=x[:, t, :],
                                                 scalar=gain("final_g", t), in1=rms[:, :],
                                                 op0=ALU.mult, op1=ALU.mult).then_inc(x_ready, 1)
                if j == 5:
                    spatial_operands()
            for ct in range(6):
                dve.wait_ge(gm_ready, ct + 1)
                for lo, hi, g in gm_parts(ct):
                    dve.scalar_tensor_tensor(
                        out=tmp[lo:hi, ct % 2, :].rearrange("p (n t) -> p n t", t=P),
                        in0=bank[4 + ct % 2][lo:hi, :].rearrange("p (n t) -> p n t", t=P),
                        scalar=vec[lo:hi, VEC0["a_v_norm_2"] + ct:VEC0["a_v_norm_2"] + ct + 1],
                        in1=bs[lo:hi, g, :].rearrange("p (o t) -> p o t", o=1)
                        .to_broadcast([hi - lo, NT, P]), op0=ALU.mult, op1=ALU.add).then_inc(gm_biased, 1)
                dve.wait_ge(gm_biased, gm_count(ct))
                dve.wait_ge(gelu_done, 4 + ct // 2)
                dve.tensor_tensor(z_a[:, ct, :], tmp[:, ct % 2, :], z_a[:, ct, :], ALU.mult)\
                    .then_inc(gm_done, 1)
                if ct:
                    gm_low(ct - 1)
            gm_low(5)
            dve.wait_ge(zero_set, 1)
            softmax("mem_a")
            out_phase("a_out", "a2", move=("up1", act_parts, lambda t: gain("a_norm2_2", t)))
            up(1)
            down(1, "b1", move=("b_q", act_parts, lambda t: gain("b_norm1_2", t)))
            for t in range(KT):
                gain_low("kv", t, (kvm_hi, kvm_lo), gain("kv_norm_2", t))
            with dve.Fori(0, 2) as i:
                for s in range(2):
                    split_w(2 * i + s + C0["b_q"] + 2, s)
                    norm_group(2 * i + s + C0["b_q"], 2 * i + s + first_tiles(G0["b_q"]), s,
                               lambda m: q_b[:, bass.ds(4 * i + 2 * s + m, 1), :], rms, HD ** -0.5)
            with dve.Fori(0, 2) as i:
                for s in range(2):
                    split_w(2 * i + s + C0["kv"] + 2, s)
                    norm_group(2 * i + s + C0["kv"], 2 * i + s + first_tiles(G0["kv"]), s,
                               lambda m: kv_b[:, bass.ds(4 * i + 2 * s + m, 1), :], rms)
            dve.wait_ge(bf_loaded, 16)
            for j in range(4):
                c = C0["kv"] + 4 + j
                split_w(c + 2, j % 2, KT * KV_TAIL[2 + j][1] if j < 2 else 2048)
                if j == 0:
                    norm_group(c, first_tiles(G0["kv"] + 4), 0, lambda m: kv_b[:, 8 + m, :], rms)
                elif j < 3:
                    dve.wait_ge(chunk_done, c + 1)
                    norm_tile(kv_b[:, 9 + j, :], bank[2 * (j % 2)], rms).then_inc(group_free, 1)
                else:
                    dve.wait_ge(chunk_done, c + 1)
                    dve.tensor_tensor(f_rows[:, 1, :], bank[2][0:FOX, :], rms[0:FOX, :], ALU.mult)\
                        .then_inc(group_free, 1)
            dve.wait_ge(group_free, G0["b_out"])
            dve.tensor_scalar(f_rows[:, 0, :], f_rows[:, 1, :], b_f, -1.0, ALU.add, ALU.mult)\
                .then_inc(f_neg, 1)
            dve.wait_ge(f_neg, 1)
            dve.tensor_scalar(f_rows[:, 2, :], f_rows[:, 0, :], CLAMP, None, ALU.min).then_inc(f_clamped, 1)
            dve.memset(triext[:, P:SEQ], 1.0).then_inc(tri_set, 1)
            dve.tensor_copy(triext[:, 0:P], tri[:, :]).then_inc(tri_set, 1)
            dve.memset(zero_b[:, :], 0.0).then_inc(zero_set, 1)
            for b in range(8):
                t, half = b // 2, b % 2
                dve.tensor_copy(vtok_b[:, t, 384 * half:384 * (half + 1)], tr_bank("v_b", b)[:, 0:384])\
                    .then_inc(tr_saved, 1)
            dve.wait_ge(f_logged, 1)
            dve.tensor_tensor(f_rows[:, 1, :], f_rows[:, 2, :], f_rows[:, 0, :], ALU.max).then_inc(f_plus, 1)
            dve.tensor_copy(lfT, tr_bank("f", 0)[:, 0:NT * FOX].rearrange("p (t f) -> p t f", f=FOX))\
                .then_inc(tr_saved, 1)
            dve.wait_ge(f_summed, 1)
            dve.tensor_copy(f_rows[:, 0, :], bank[4][0:FOX, :]).then_inc(f_saved, 1)
            dve.wait_ge(decay_back, 16)
            softmax("fox")
            dve.wait_ge(zero_set, 2)
            softmax("mem_b")
            out_phase("b_out", "b2", move=("up2", act_parts, lambda t: gain("b_norm2_2", t)))
            up(2)
            down(2, "final")
            for t in range(KT):
                dve.scalar_tensor_tensor(out=y[:, t, :], in0=x[:, t, :], scalar=gain("final_norm_2", t),
                                         in1=rms[:, :], op0=ALU.mult, op1=ALU.mult).then_inc(y_ready, 1)
            for b in range(8):
                t, half = b // 2, b % 2
                dve.tensor_copy(y_tok[:, t, 512 * half:512 * (half + 1)], tr_bank("out", b)[:, :])\
                    .then_inc(tr_saved, 1)


INPUTS = ["x", "c", "w_ada", "b_ada", "w_in", "rel_bias", "g_a", "g_b", "w_out", "w_up", "conv_w",
          "conv_b", "w_down", "final_g", "mem_2", "a_norm1_2", "a_w_in_2", "a_v_norm_2", "a_w_s_2",
          "a_b_s_2", "a_mem_norm_2", "a_w_mem_kv_2", "a_w_out_2", "a_norm2_2", "a_ffn_in_2",
          "a_ffn_conv_2", "a_ffn_conv_b_2", "a_ffn_out_2", "kv_norm_2", "w_kv_2", "b_f_2",
          "b_norm1_2", "b_w_q_2", "b_mem_norm_2", "b_w_mem_kv_2", "b_w_out_2", "b_norm2_2",
          "b_ffn_in_2", "b_ffn_conv_2", "b_ffn_conv_b_2", "b_ffn_out_2", "final_norm_2"]


def kernel(**inputs):
    import numpy as np
    import concourse.bacc as bacc
    from concourse.bass_utils import run_bass_kernel_spmd

    nc = bacc.Bacc("TRN2", target_bir_lowering=False, num_devices=1)
    arrays, aps = {}, {}
    for name in INPUTS:
        v = np.ascontiguousarray(inputs[name])
        arrays["in_" + name] = v
        aps[name] = nc.dram_tensor("in_" + name, v.shape, mybir.dt.from_np(v.dtype),
                                   kind="ExternalInput").ap()
    out = nc.dram_tensor("out_x", (1, SEQ, D), FP32, kind="ExternalOutput").ap()
    program(nc, aps, out)
    r = run_bass_kernel_spmd(nc, [arrays], core_ids=[0])
    return r.results[0]["out_x"]
```
